# Optimizing a Trainium2 kernel written in Bass

```python
import jax, jax.numpy as jnp
from jax import lax
import numpy as np
import math, functools

D_MODEL = 1024
BATCH = 1
SEQ = 512
DEPTH = 2

FOX_HEADS = 8
FOX_HEAD_DIM = 64
FOX_WIDTH = FOX_HEADS * FOX_HEAD_DIM
RET_HEADS = 4
RET_HEAD_DIM = 128
RET_WIDTH = RET_HEADS * RET_HEAD_DIM
MIX_WIDTH = FOX_WIDTH + RET_WIDTH
IN_COLS = 3 * FOX_WIDTH + FOX_HEADS + 4 * RET_WIDTH
D_FF = 4 * D_MODEL
Q_BLOCK = 128
RET_CHUNK = 128
ROPE_BASE = 10000.0
LN_EPS = 1e-5
GN_EPS = 1e-5
DEEPNORM_ALPHA = (2 * DEPTH) ** 0.25
DEEPNORM_BETA = (8 * DEPTH) ** -0.25


SPLITS = [FOX_WIDTH, 2 * FOX_WIDTH, 3 * FOX_WIDTH, 3 * FOX_WIDTH + FOX_HEADS,
          3 * FOX_WIDTH + FOX_HEADS + RET_WIDTH, 3 * FOX_WIDTH + FOX_HEADS + 2 * RET_WIDTH,
          3 * FOX_WIDTH + FOX_HEADS + 3 * RET_WIDTH]

def layernorm(x, g, b):
    xf = x.astype(jnp.float32)
    mu = jnp.mean(xf, axis=-1, keepdims=True)
    var = jnp.mean(jnp.square(xf - mu), axis=-1, keepdims=True)
    y = (xf - mu) * lax.rsqrt(var + LN_EPS)
    return (y * g + b).astype(x.dtype)

def rotary(x):
    s, d = x.shape[1], x.shape[-1]
    half = d // 2
    inv_freq = ROPE_BASE ** (-jnp.arange(half, dtype=jnp.float32) / half)
    ang = jnp.arange(s, dtype=jnp.float32)[:, None] * inv_freq[None, :]
    cos = jnp.cos(ang)[None, :, None, :]
    sin = jnp.sin(ang)[None, :, None, :]
    x1, x2 = x[..., :half].astype(jnp.float32), x[..., half:].astype(jnp.float32)
    return jnp.concatenate([x1 * cos - x2 * sin, x1 * sin + x2 * cos], axis=-1).astype(x.dtype)

def fox_attention(q, k, v, log_f):
    b, s, h, d = q.shape
    n_blocks = s // Q_BLOCK
    scale = d ** -0.5
    c = jnp.cumsum(log_f.astype(jnp.float32), axis=1).transpose(0, 2, 1)
    qb = q.reshape(b, n_blocks, Q_BLOCK, h, d).transpose(1, 0, 2, 3, 4)
    cb = c.reshape(b, h, n_blocks, Q_BLOCK).transpose(2, 0, 1, 3)
    key_pos = jnp.arange(s)

    def block(args):
        i, q_i, c_i = args
        scores = jnp.einsum('bqhd,bkhd->bhqk', q_i, k).astype(jnp.float32) * scale
        bias = c_i[..., :, None] - c[..., None, :]
        q_pos = i * Q_BLOCK + jnp.arange(Q_BLOCK)
        causal = key_pos[None, :] <= q_pos[:, None]
        logits = jnp.where(causal, scores + bias, -jnp.inf)
        p = jax.nn.softmax(logits, axis=-1)
        return jnp.einsum('bhqk,bkhd->bqhd', p.astype(v.dtype), v)

    out = lax.map(block, (jnp.arange(n_blocks), qb, cb))
    return out.transpose(1, 0, 2, 3, 4).reshape(b, s, h * d)

def retention_chunkwise(q, k, v, gamma):
    b, s, h, dk = q.shape
    dv = v.shape[-1]
    n_chunks = s // RET_CHUNK
    log_g = jnp.log(gamma)
    idx = jnp.arange(RET_CHUNK, dtype=jnp.float32)
    diff = idx[:, None] - idx[None, :]
    decay_mask = jnp.where(diff >= 0,
                           jnp.exp(log_g[:, None, None] * jnp.maximum(diff, 0.0)), 0.0)
    xi = jnp.exp(log_g[:, None] * (idx + 1.0))[..., None]
    zeta = jnp.exp(log_g[:, None] * (RET_CHUNK - 1.0 - idx))[..., None]
    chunk_decay = jnp.exp(log_g * RET_CHUNK)[:, None, None]

    def to_chunks(t):
        return t.reshape(b, n_chunks, RET_CHUNK, h, t.shape[-1]).transpose(1, 0, 3, 2, 4)

    def step(state, inp):
        q_i, k_i, v_i = inp
        inner = jnp.einsum('bhqd,bhkd->bhqk', q_i, k_i) * decay_mask
        o = (jnp.einsum('bhqk,bhkv->bhqv', inner, v_i)
             + jnp.einsum('bhqd,bhdv->bhqv', q_i * xi, state))
        state = chunk_decay * state + jnp.einsum('bhkd,bhkv->bhdv', k_i * zeta, v_i)
        return state, o

    state0 = jnp.zeros((b, h, dk, dv), jnp.float32)
    _, out = lax.scan(step, state0, (to_chunks(q), to_chunks(k), to_chunks(v)))
    return out.transpose(1, 0, 3, 2, 4).reshape(b, s, h, dv)

def head_groupnorm(x, g):
    xf = x.astype(jnp.float32)
    mu = jnp.mean(xf, axis=-1, keepdims=True)
    var = jnp.mean(jnp.square(xf - mu), axis=-1, keepdims=True)
    return ((xf - mu) * lax.rsqrt(var + GN_EPS) * g).astype(x.dtype)

def hybrid_layer(x, w_in, w_out, w_ff1, w_ff2, ln1_g, ln1_b, ln2_g, ln2_b, b_forget, ret_gn_g, gamma):
    b, s, _ = x.shape
    proj = jnp.einsum('bsd,dc->bsc', x, w_in)
    fq, fk, fv, f_logit, rq, rk, rv, rg = jnp.split(proj, SPLITS, axis=-1)

    fshape = (b, s, FOX_HEADS, FOX_HEAD_DIM)
    log_f = jax.nn.log_sigmoid((f_logit + b_forget).astype(jnp.float32))
    fox_out = fox_attention(fq.reshape(fshape), fk.reshape(fshape), fv.reshape(fshape), log_f)

    rshape = (b, s, RET_HEADS, RET_HEAD_DIM)
    q_r = rotary(rq.reshape(rshape))
    k_r = rotary(rk.reshape(rshape)) * (RET_HEAD_DIM ** -0.5)
    ret = retention_chunkwise(q_r, k_r, rv.reshape(rshape), gamma)
    ret = head_groupnorm(ret, ret_gn_g).reshape(b, s, RET_WIDTH).astype(x.dtype)
    ret_out = jax.nn.silu(rg) * ret

    mixed = jnp.concatenate([fox_out.astype(x.dtype), ret_out], axis=-1)
    mix = jnp.einsum('bsc,cd->bsd', mixed, w_out)
    x = layernorm(DEEPNORM_ALPHA * x + mix, ln1_g, ln1_b)

    hid = jnp.square(jax.nn.relu(jnp.einsum('bsd,df->bsf', x, w_ff1)))
    ff = jnp.einsum('bsf,fd->bsd', hid, w_ff2)
    return layernorm(DEEPNORM_ALPHA * x + ff, ln2_g, ln2_b)

def first_inputs(seed: int = 0) -> dict:
    key = jax.random.key(seed)
    ks = jax.random.split(key, 12)
    f32 = jnp.float32
    x = jax.random.normal(ks[0], (BATCH, SEQ, D_MODEL), f32)
    w_in = jax.random.normal(ks[1], (DEPTH, D_MODEL, IN_COLS), f32) * D_MODEL ** -0.5
    col = jnp.arange(IN_COLS)
    is_value = (((col >= SPLITS[1]) & (col < SPLITS[2]))
                | ((col >= SPLITS[5]) & (col < SPLITS[6])))
    w_in = w_in * jnp.where(is_value, DEEPNORM_BETA, 1.0).astype(f32)
    w_out = jax.random.normal(ks[2], (DEPTH, MIX_WIDTH, D_MODEL), f32) * (MIX_WIDTH ** -0.5 * DEEPNORM_BETA)
    w_ff1 = jax.random.normal(ks[3], (DEPTH, D_MODEL, D_FF), f32) * (D_MODEL ** -0.5 * DEEPNORM_BETA)
    w_ff2 = jax.random.normal(ks[4], (DEPTH, D_FF, D_MODEL), f32) * (D_FF ** -0.5 * DEEPNORM_BETA)
    ln1_g = 1.0 + 0.02 * jax.random.normal(ks[5], (DEPTH, D_MODEL), f32)
    ln1_b = 0.02 * jax.random.normal(ks[6], (DEPTH, D_MODEL), f32)
    ln2_g = 1.0 + 0.02 * jax.random.normal(ks[7], (DEPTH, D_MODEL), f32)
    ln2_b = 0.02 * jax.random.normal(ks[8], (DEPTH, D_MODEL), f32)
    b_forget = jax.random.uniform(ks[9], (DEPTH, FOX_HEADS), f32, 1.0, 5.0)
    ret_gn_g = 1.0 + 0.02 * jax.random.normal(ks[10], (DEPTH, RET_HEADS, RET_HEAD_DIM), f32)
    return {"x": x, "w_in": w_in, "w_out": w_out, "w_ff1": w_ff1, "w_ff2": w_ff2,
            "ln1_g": ln1_g, "ln1_b": ln1_b, "ln2_g": ln2_g, "ln2_b": ln2_b,
            "b_forget": b_forget, "ret_gn_g": ret_gn_g}

def first_block(x, w_in, w_out, w_ff1, w_ff2, ln1_g, ln1_b, ln2_g, ln2_b, b_forget, ret_gn_g):
    gamma = 1.0 - jnp.exp2(-5.0 - jnp.arange(RET_HEADS, dtype=jnp.float32))
    for layer in range(DEPTH):
        x = hybrid_layer(x, w_in[layer], w_out[layer], w_ff1[layer], w_ff2[layer],
                         ln1_g[layer], ln1_b[layer], ln2_g[layer], ln2_b[layer],
                         b_forget[layer], ret_gn_g[layer], gamma)
    return x


DEPTH_2 = 1

N_MIXERS = 3
HEAD_DIM = 64
N_HEADS = D_MODEL // HEAD_DIM
REL_BUCKETS = 32
REL_MAX_DIST = 2048
GLA_HEADS = 4
GLA_DK = D_MODEL // 2 // GLA_HEADS
GLA_DV = D_MODEL // GLA_HEADS
GLA_GATE_RANK = 16
GLA_TAU = 16.0
GLA_CHUNK = 64
GLA_IN = 2 * GLA_HEADS * GLA_DK + 2 * GLA_HEADS * GLA_DV + GLA_GATE_RANK
NSA_KV_GROUPS = 4
NSA_Q_PER_KV = N_HEADS // NSA_KV_GROUPS
CMP_LEN = 32
CMP_STRIDE = 16
CMP_HIDDEN = 256
SEL_LEN = 64
SEL_TOP = 16
WIN_LEN = 512
NSA_IN = N_HEADS * HEAD_DIM + 6 * NSA_KV_GROUPS * HEAD_DIM + 3 * N_HEADS
DIL_GROUPS = ((128, 1), (512, 4), (2048, 16))
DIL_IN = len(DIL_GROUPS) * 3 * N_HEADS * HEAD_DIM
D_FF_2 = 2816
CONV_W = 3
DN_ALPHA = (2 * DEPTH_2) ** 0.25
DN_BETA = (8 * DEPTH_2) ** -0.25


def layer_norm(x, g, b):
    xf = x.astype(jnp.float32)
    mu = jnp.mean(xf, -1, keepdims=True)
    var = jnp.mean(jnp.square(xf - mu), -1, keepdims=True)
    return ((xf - mu) * lax.rsqrt(var + LN_EPS) * g + b).astype(x.dtype)

def rel_bucket(dist):
    n = jnp.maximum(dist, 0)
    exact = REL_BUCKETS // 2
    logn = jnp.log(jnp.maximum(n, 1).astype(jnp.float32) / exact)
    large = exact + (logn / math.log(REL_MAX_DIST / exact) * (REL_BUCKETS - exact)).astype(jnp.int32)
    large = jnp.minimum(large, REL_BUCKETS - 1)
    return jnp.where(n < exact, n, large)

def masked_softmax(s, mask):
    s = jnp.where(mask, s.astype(jnp.float32), -jnp.inf)
    m = jnp.max(s, axis=-1, keepdims=True)
    m = jnp.where(jnp.isfinite(m), m, 0.0)
    e = jnp.where(mask, jnp.exp(s - m), 0.0)
    den = jnp.sum(e, axis=-1, keepdims=True)
    p = e / jnp.where(den > 0, den, 1.0)
    return p, (m + jnp.log(den))[..., 0]

def banded_attention(q, k, v, max_dist, dist_scale, rel_table):
    n, l, g, r, dh = q.shape
    nblk = -(-l // Q_BLOCK)
    lp = nblk * Q_BLOCK
    nb = -(-max_dist // Q_BLOCK)
    span = (nb + 1) * Q_BLOCK
    qp = jnp.pad(q, ((0, 0), (0, lp - l), (0, 0), (0, 0), (0, 0)))
    kv_pad = ((0, 0), (nb * Q_BLOCK, lp - l), (0, 0), (0, 0))
    kp = jnp.pad(k, kv_pad)
    vp = jnp.pad(v, kv_pad)
    dist = jnp.arange(Q_BLOCK)[:, None] - jnp.arange(span)[None, :] + nb * Q_BLOCK
    band = (dist >= 0) & (dist <= max_dist)
    bias = rel_table[rel_bucket(dist * dist_scale)].reshape(Q_BLOCK, span, g, r)
    bias = bias.transpose(2, 3, 0, 1).astype(jnp.float32)
    scale = dh ** -0.5

    def block(i):
        q0 = i * Q_BLOCK
        qi = lax.dynamic_slice_in_dim(qp, q0, Q_BLOCK, axis=1)
        ki = lax.dynamic_slice_in_dim(kp, q0, span, axis=1)
        vi = lax.dynamic_slice_in_dim(vp, q0, span, axis=1)
        kpos = q0 - nb * Q_BLOCK + jnp.arange(span)
        mask = band & (kpos >= 0)[None, :]
        s = jnp.einsum('nqgrd,nkgd->ngrqk', qi, ki).astype(jnp.float32) * scale + bias
        p, lse = masked_softmax(s, mask)
        o = jnp.einsum('ngrqk,nkgd->nqgrd', p.astype(vi.dtype), vi)
        return o, lse

    o, lse = lax.map(block, jnp.arange(nblk))
    o = jnp.moveaxis(o, 0, 1).reshape(n, lp, g, r, dh)[:, :l]
    lse = lse.transpose(1, 0, 4, 2, 3).reshape(n, lp, g, r)[:, :l]
    return o, lse

def gla_mixer(h, w_in, w_a2, b_a, norm_g, w_o):
    b, s, _ = h.shape
    qk, dv = GLA_HEADS * GLA_DK, GLA_HEADS * GLA_DV
    q, k, v, r, a_lr = jnp.split(h @ w_in, [qk, 2 * qk, 2 * qk + dv, 2 * qk + 2 * dv], axis=-1)
    log_a = jax.nn.log_sigmoid((a_lr @ w_a2 + b_a).astype(jnp.float32)) / GLA_TAU
    nc = s // GLA_CHUNK

    def chunks(t, d):
        return t.astype(jnp.float32).reshape(b, nc, GLA_CHUNK, GLA_HEADS, d).transpose(0, 3, 1, 2, 4)

    qf = chunks(q, GLA_DK) * GLA_DK ** -0.5
    kf = chunks(k, GLA_DK)
    vf = chunks(v, GLA_DV)
    bcum = jnp.cumsum(chunks(log_a, GLA_DK), axis=3)
    blast = bcum[:, :, :, -1:, :]
    q_dec = qf * jnp.exp(bcum)
    k_inv = kf * jnp.exp(-bcum)
    k_dec = kf * jnp.exp(blast - bcum)
    causal = jnp.tril(jnp.ones((GLA_CHUNK, GLA_CHUNK), dtype=bool))
    att = jnp.where(causal, jnp.einsum('bhnid,bhnjd->bhnij', q_dec, k_inv), 0.0)
    o_intra = jnp.einsum('bhnij,bhnje->bhnie', att, vf)

    def step(state, xs):
        qc, kc, vc, dl = xs
        o = jnp.einsum('bhcd,bhde->bhce', qc, state)
        state = state * dl[..., None] + jnp.einsum('bhcd,bhce->bhde', kc, vc)
        return state, o

    xs = (jnp.moveaxis(q_dec, 2, 0), jnp.moveaxis(k_dec, 2, 0), jnp.moveaxis(vf, 2, 0),
          jnp.moveaxis(jnp.exp(blast[:, :, :, 0]), 2, 0))
    state0 = jnp.zeros((b, GLA_HEADS, GLA_DK, GLA_DV), jnp.float32)
    _, o_inter = lax.scan(step, state0, xs)
    o = o_intra + jnp.moveaxis(o_inter, 0, 2)
    o = o * lax.rsqrt(jnp.mean(o * o, -1, keepdims=True) + LN_EPS) * norm_g
    o = o.transpose(0, 2, 3, 1, 4).reshape(b, s, dv).astype(h.dtype)
    return (o * jax.nn.silu(r)) @ w_o

def compress(x, pe, w1, b1, w2):
    b, s, g, dh = x.shape
    ratio = CMP_LEN // CMP_STRIDE
    pieces = x.reshape(b, s // CMP_STRIDE, CMP_STRIDE, g, dh)
    nc = s // CMP_STRIDE - ratio + 1
    blocks = jnp.concatenate([pieces[:, j:j + nc] for j in range(ratio)], axis=2)
    blocks = (blocks + pe[:, None, :]).transpose(0, 1, 3, 2, 4).reshape(b, nc, g, CMP_LEN * dh)
    return jax.nn.silu(blocks @ w1 + b1) @ w2

def nsa_cmp_sel(q, kcmp, vcmp, ks, vs, rel_table):
    b, s, G, R, dh = q.shape
    nc = kcmp.shape[1]
    nsel = s // SEL_LEN
    top = min(SEL_TOP, nsel)
    ratio_sel = SEL_LEN // CMP_STRIDE
    ratio_cmp = CMP_LEN // CMP_STRIDE
    scale = dh ** -0.5
    cmp_end = jnp.arange(nc) * CMP_STRIDE + CMP_LEN - 1
    ks_blk = ks.reshape(b, nsel, SEL_LEN, G, dh).transpose(0, 3, 1, 2, 4)
    vs_blk = vs.reshape(b, nsel, SEL_LEN, G, dh).transpose(0, 3, 1, 2, 4)
    tab_g = rel_table.reshape(REL_BUCKETS, G, R).transpose(1, 0, 2).reshape(G * REL_BUCKETS, R)
    b_ix = jnp.arange(b)[:, None, None, None]
    g_ix = jnp.arange(G)[None, :, None, None]
    blk_ids = jnp.arange(nsel)[None, :]

    def block(i):
        t = i * Q_BLOCK + jnp.arange(Q_BLOCK)
        qi = lax.dynamic_slice_in_dim(q, i * Q_BLOCK, Q_BLOCK, axis=1)
        dist_c = t[:, None] - cmp_end[None, :]
        bias_c = rel_table[rel_bucket(dist_c)].reshape(Q_BLOCK, nc, G, R).transpose(2, 3, 0, 1)
        s_c = jnp.einsum('bqgrd,bjgd->bgrqj', qi, kcmp).astype(jnp.float32) * scale + bias_c
        p_c, _ = masked_softmax(s_c, dist_c >= 0)
        o_c = jnp.einsum('bgrqj,bjgd->bqgrd', p_c.astype(vcmp.dtype), vcmp)
        p_g = jnp.pad(p_c.sum(axis=2), ((0, 0), (0, 0), (0, 0), (ratio_cmp - 1, ratio_sel * nsel - nc)))
        imp = jnp.stack([p_g[..., m - n + ratio_cmp - 1: m - n + ratio_cmp - 1 + ratio_sel * nsel: ratio_sel]
                         for m in range(ratio_sel) for n in range(ratio_cmp)]).sum(0)
        cur = (t // SEL_LEN)[:, None]
        valid = blk_ids * SEL_LEN <= t[:, None]
        forced = (blk_ids == 0) | (blk_ids == cur) | (blk_ids == cur - 1)
        score = jnp.where(valid, jnp.where(forced, jnp.inf, imp), -jnp.inf)
        top_s, idx = lax.top_k(score, top)
        k_sel = ks_blk[b_ix, g_ix, idx].reshape(b, G, Q_BLOCK, top * SEL_LEN, dh)
        v_sel = vs_blk[b_ix, g_ix, idx].reshape(b, G, Q_BLOCK, top * SEL_LEN, dh)
        pos = (idx[..., None] * SEL_LEN + jnp.arange(SEL_LEN)).reshape(b, G, Q_BLOCK, top * SEL_LEN)
        dist_s = t[None, None, :, None] - pos
        mask_s = jnp.repeat(top_s > -jnp.inf, SEL_LEN, axis=-1) & (dist_s >= 0)
        bias_s = tab_g[g_ix * REL_BUCKETS + rel_bucket(dist_s)].transpose(0, 1, 4, 2, 3)
        s_s = jnp.einsum('bqgrd,bgqkd->bgrqk', qi, k_sel).astype(jnp.float32) * scale + bias_s
        p_s, _ = masked_softmax(s_s, mask_s[:, :, None])
        o_s = jnp.einsum('bgrqk,bgqkd->bqgrd', p_s.astype(v_sel.dtype), v_sel)
        return o_c, o_s

    o_c, o_s = lax.map(block, jnp.arange(s // Q_BLOCK))
    o_c = jnp.moveaxis(o_c, 0, 1).reshape(b, s, G, R, dh)
    o_s = jnp.moveaxis(o_s, 0, 1).reshape(b, s, G, R, dh)
    return o_c, o_s

def nsa_mixer(h, w_in, cmp_pe, cmp_w1, cmp_b1, cmp_w2, rel_table, w_o):
    b, s, _ = h.shape
    G, R, dh = NSA_KV_GROUPS, NSA_Q_PER_KV, HEAD_DIM
    splits = np.cumsum([N_HEADS * dh] + [G * dh] * 6).tolist()
    q, kc, vc, ks, vs, kw, vw, gates = jnp.split(h @ w_in, splits, axis=-1)
    q = q.reshape(b, s, G, R, dh)
    kc, vc, ks, vs, kw, vw = (t.reshape(b, s, G, dh) for t in (kc, vc, ks, vs, kw, vw))
    kcmp = compress(kc, cmp_pe[0], cmp_w1[0], cmp_b1[0], cmp_w2[0])
    vcmp = compress(vc, cmp_pe[1], cmp_w1[1], cmp_b1[1], cmp_w2[1])
    o_cmp, o_sel = nsa_cmp_sel(q, kcmp, vcmp, ks, vs, rel_table)
    o_win, _ = banded_attention(q, kw, vw, WIN_LEN - 1, 1, rel_table)
    gt = jax.nn.sigmoid(gates.astype(jnp.float32)).reshape(b, s, 3, G, R, 1).astype(h.dtype)
    o = gt[:, :, 0] * o_cmp + gt[:, :, 1] * o_sel + gt[:, :, 2] * o_win
    return o.reshape(b, s, N_HEADS * dh) @ w_o

def dilated_mixer(h, w_in, rel_table, w_o):
    b, s, d_model = h.shape
    hd = N_HEADS * HEAD_DIM
    w_g = w_in.reshape(d_model, len(DIL_GROUPS), 3, hd)
    outs, lses = [], []
    for gi, (window, dil) in enumerate(DIL_GROUPS):
        qkv = jnp.einsum('bsd,dce->bsce', h, w_g[:, gi])
        lsub = s // dil

        def by_residue(t):
            return t.reshape(b, lsub, dil, N_HEADS, HEAD_DIM).transpose(0, 2, 1, 3, 4).reshape(b * dil, lsub, N_HEADS, HEAD_DIM)

        o, lse = banded_attention(by_residue(qkv[:, :, 0])[:, :, :, None], by_residue(qkv[:, :, 1]),
                                  by_residue(qkv[:, :, 2]), window // dil, dil, rel_table)
        o = o[:, :, :, 0].reshape(b, dil, lsub, N_HEADS, HEAD_DIM).transpose(0, 2, 1, 3, 4).reshape(b, s, N_HEADS, HEAD_DIM)
        lse = lse[..., 0].reshape(b, dil, lsub, N_HEADS).transpose(0, 2, 1, 3).reshape(b, s, N_HEADS)
        outs.append(o)
        lses.append(lse)
    wts = jax.nn.softmax(jnp.stack(lses, axis=-1), axis=-1).astype(h.dtype)
    o = jnp.einsum('bshg,bshgd->bshd', wts, jnp.stack(outs, axis=3))
    return o.reshape(b, s, hd) @ w_o

def conv_ffn(h, w_up, conv_w, conv_b, w_down):
    u, g = jnp.split(h @ w_up, 2, axis=-1)
    u = lax.conv_general_dilated(u, conv_w[:, None, :], window_strides=(1,), padding=((CONV_W - 1, 0),),
                                 dimension_numbers=('NWC', 'WIO', 'NWC'), feature_group_count=D_FF_2) + conv_b
    return (jax.nn.silu(u) * g) @ w_down

def post_norm_residual(x, cs, w_mod, b_mod, ln_gain, ln_bias, sublayer):
    shift, scale, gate = jnp.split((cs @ w_mod + b_mod)[:, None, :], 3, axis=-1)
    y = sublayer(x * (1 + scale) + shift)
    return layer_norm(DN_ALPHA * x + (1 + gate) * y, ln_gain, ln_bias)

def second_inputs(seed: int = 0) -> dict:
    key = jax.random.key(seed)
    keys = iter(jax.random.split(key, 32))

    def nrm(shape, std):
        return std * jax.random.normal(next(keys), shape, jnp.float32)

    n_a, n_b, n_c = (len(range(m, DEPTH_2, N_MIXERS)) for m in range(N_MIXERS))
    D = D_MODEL
    hd = N_HEADS * HEAD_DIM
    return {
        'x': nrm((BATCH, SEQ, D), 1.0),
        'c': nrm((BATCH, D), 1.0),
        'rel_table': nrm((REL_BUCKETS, N_HEADS), 0.5),
        'mod_w': nrm((DEPTH_2, 2, D, 3 * D), 0.5 * D ** -0.5),
        'mod_b': nrm((DEPTH_2, 2, 3 * D), 0.02),
        'ln_g': 1.0 + nrm((DEPTH_2, 2, D), 0.02),
        'ln_b': nrm((DEPTH_2, 2, D), 0.02),
        'gla_w_in': nrm((n_a, D, GLA_IN), D ** -0.5),
        'gla_w_a2': nrm((n_a, GLA_GATE_RANK, GLA_HEADS * GLA_DK), GLA_GATE_RANK ** -0.5),
        'gla_b_a': nrm((n_a, GLA_HEADS * GLA_DK), 0.1),
        'gla_norm_g': 1.0 + nrm((n_a, GLA_DV), 0.02),
        'gla_w_o': nrm((n_a, GLA_HEADS * GLA_DV, D), DN_BETA * (GLA_HEADS * GLA_DV) ** -0.5),
        'nsa_w_in': nrm((n_b, D, NSA_IN), D ** -0.5),
        'nsa_cmp_pe': nrm((n_b, 2, CMP_LEN, HEAD_DIM), 0.1),
        'nsa_cmp_w1': nrm((n_b, 2, CMP_LEN * HEAD_DIM, CMP_HIDDEN), (CMP_LEN * HEAD_DIM) ** -0.5),
        'nsa_cmp_b1': nrm((n_b, 2, CMP_HIDDEN), 0.02),
        'nsa_cmp_w2': nrm((n_b, 2, CMP_HIDDEN, HEAD_DIM), CMP_HIDDEN ** -0.5),
        'nsa_w_o': nrm((n_b, hd, D), DN_BETA * hd ** -0.5),
        'dil_w_in': nrm((n_c, D, DIL_IN), D ** -0.5),
        'dil_w_o': nrm((n_c, hd, D), DN_BETA * hd ** -0.5),
        'ffn_w_up': nrm((DEPTH_2, D, 2 * D_FF_2), D ** -0.5),
        'ffn_conv_w': nrm((DEPTH_2, CONV_W, D_FF_2), CONV_W ** -0.5),
        'ffn_conv_b': nrm((DEPTH_2, D_FF_2), 0.02),
        'ffn_w_down': nrm((DEPTH_2, D_FF_2, D), DN_BETA * D_FF_2 ** -0.5),
    }

def second_block(x, c, rel_table, mod_w, mod_b, ln_g, ln_b,
              gla_w_in, gla_w_a2, gla_b_a, gla_norm_g, gla_w_o,
              nsa_w_in, nsa_cmp_pe, nsa_cmp_w1, nsa_cmp_b1, nsa_cmp_w2, nsa_w_o,
              dil_w_in, dil_w_o,
              ffn_w_up, ffn_conv_w, ffn_conv_b, ffn_w_down):
    cs = jax.nn.silu(c)
    for i in range(DEPTH_2):
        kind, j = i % N_MIXERS, i // N_MIXERS
        if kind == 0:
            mixer = functools.partial(gla_mixer, w_in=gla_w_in[j], w_a2=gla_w_a2[j], b_a=gla_b_a[j],
                                      norm_g=gla_norm_g[j], w_o=gla_w_o[j])
        elif kind == 1:
            mixer = functools.partial(nsa_mixer, w_in=nsa_w_in[j], cmp_pe=nsa_cmp_pe[j], cmp_w1=nsa_cmp_w1[j],
                                      cmp_b1=nsa_cmp_b1[j], cmp_w2=nsa_cmp_w2[j], rel_table=rel_table,
                                      w_o=nsa_w_o[j])
        else:
            mixer = functools.partial(dilated_mixer, w_in=dil_w_in[j], rel_table=rel_table, w_o=dil_w_o[j])
        x = post_norm_residual(x, cs, mod_w[i, 0], mod_b[i, 0], ln_g[i, 0], ln_b[i, 0], mixer)
        ffn = functools.partial(conv_ffn, w_up=ffn_w_up[i], conv_w=ffn_conv_w[i], conv_b=ffn_conv_b[i],
                                w_down=ffn_w_down[i])
        x = post_norm_residual(x, cs, mod_w[i, 1], mod_b[i, 1], ln_g[i, 1], ln_b[i, 1], ffn)
    return x


def setup_inputs(seed=0):
    out = dict(first_inputs(seed))
    for name, value in second_inputs(seed + 1).items():
        if name != "x":
            out[name + "_2"] = value
    return out


def reference(
    x, w_in, w_out, w_ff1, w_ff2, ln1_g, ln1_b, ln2_g, ln2_b, b_forget, ret_gn_g, c_2,
    rel_table_2, mod_w_2, mod_b_2, ln_g_2, ln_b_2, gla_w_in_2, gla_w_a2_2, gla_b_a_2,
    gla_norm_g_2, gla_w_o_2, nsa_w_in_2, nsa_cmp_pe_2, nsa_cmp_w1_2, nsa_cmp_b1_2, nsa_cmp_w2_2,
    nsa_w_o_2, dil_w_in_2, dil_w_o_2, ffn_w_up_2, ffn_conv_w_2, ffn_conv_b_2, ffn_w_down_2,
):
    x = first_block(
        x, w_in, w_out, w_ff1, w_ff2, ln1_g, ln1_b, ln2_g, ln2_b, b_forget, ret_gn_g,
    )
    return second_block(
        x, c_2, rel_table_2, mod_w_2, mod_b_2, ln_g_2, ln_b_2, gla_w_in_2, gla_w_a2_2,
        gla_b_a_2, gla_norm_g_2, gla_w_o_2, nsa_w_in_2, nsa_cmp_pe_2, nsa_cmp_w1_2,
        nsa_cmp_b1_2, nsa_cmp_w2_2, nsa_w_o_2, dil_w_in_2, dil_w_o_2, ffn_w_up_2, ffn_conv_w_2,
        ffn_conv_b_2, ffn_w_down_2,
    )


_drawn_inputs = setup_inputs


def setup_inputs(seed=0):
    import zlib

    import numpy as np

    out = dict(_drawn_inputs(seed))
    spreads = {}
    factors = {'ret_gn_g': 8.0, 'gla_b_a_2': 3.616, 'gla_norm_g_2': 21.704, 'ffn_conv_b_2': 8.0}
    for name, (base, spread) in spreads.items():
        noise = np.random.default_rng([zlib.crc32(name.encode()), seed]).standard_normal(out[name].shape)
        drawn = base * np.exp(spread * noise) if base else spread * noise
        out[name] = __import__('jax').numpy.asarray(drawn.astype(out[name].dtype))
    for name, factor in factors.items():
        out[name] = (out[name] * factor).astype(out[name].dtype)
    return out
```

```python
from contextlib import ExitStack, contextmanager

import numpy as np

import concourse.bass as bass
from concourse import mybir

F32 = mybir.dt.float32
F32R = mybir.dt.float32r
BF16 = mybir.dt.bfloat16
I32 = mybir.dt.int32
ALU = mybir.AluOpType
ACT = mybir.ActivationFunctionType

P = 128
S = 512
NT = S // P
D = 1024
KD = D // P
HALF = 512
LAYERS = 2
FOX_H, FOX_D = 8, 64
RET_H, RET_D = 4, 128
FF = 4 * D
KF = FF // P // 2
GLA_H, GLA_DK, GLA_DV, GLA_C, GLA_RANK = 4, 128, 256, 64, 16
GLA_TAU = 16.0
NC = S // GLA_C
FF2 = 2816
KF2 = (12, 10)
UNIT = 1024
RING = 4
MOD_SLOTS = 4
EPS = 1e-5
ALPHA_1 = float((2 * LAYERS) ** 0.25)
ALPHA_2 = float(2 ** 0.25)
FOX_SCALE = FOX_D ** -0.5
MASKED = -1e30
ROW_OFF = [0, 128, 384, 768]
COL_OFF = [0, 512, 896, 1152]
PACKED = 1280
MOD_GROUPS = 6


class Steps:

    def __init__(self, engine, per_turn):
        self.engine, self.per_turn = engine, per_turn
        self.count, self.loops, self.loops_made = {}, [], 0

    def skip(self, sem, by=1):
        self.count[sem.name] = self.count.get(sem.name, 0) + by

    def at(self, sem, more=0):
        value = self.count.get(sem.name, 0) + more
        for number, i in self.loops:
            turn = self.per_turn.get((self.engine, number, sem.name), 0)
            if turn:
                value = i * turn + value
        return value

    def up(self, sem, by=1):
        self.skip(sem, by)
        return self.at(sem)

    @contextmanager
    def loop(self, eng, turns):
        number, before = self.loops_made, dict(self.count)
        self.loops_made += 1
        with eng.Fori(0, turns) as i:
            self.loops.append((number, i))
            yield i
            self.loops.pop()
        for name, n in list(self.count.items()):
            turn = n - before.get(name, 0)
            self.per_turn[(self.engine, number, name)] = turn
            self.count[name] = before.get(name, 0) + turns * turn


def program(nc, t, per_turn):
    n_units = t["stream"].shape[0]
    ctx = ExitStack()
    with ctx:
        def sb(name, shape, dt=F32):
            return ctx.enter_context(nc.sbuf_tensor(name, shape, dt))

        def sem(name):
            return ctx.enter_context(nc.semaphore(name))

        raw = sb("raw", [P, RING, UNIT])
        w_hi = sb("w_hi", [P, RING, UNIT], F32R)
        w_lo = sb("w_lo", [P, RING, UNIT], F32R)
        x = sb("x", [P, NT, D])
        xT_hi = sb("xT_hi", [P, KD, S], F32R)
        xT_lo = sb("xT_lo", [P, KD, S], F32R)
        ident = sb("ident", [P, P])
        masks = sb("masks", [P, 2 * P])
        ident_b = sb("ident_b", [P, P], BF16)
        mask_b = sb("mask_b", [P, P], BF16)
        cos_t = sb("cos_t", [P, NT, RET_D // 2])
        sin_t = sb("sin_t", [P, NT, 2, RET_D // 2])
        ones = sb("ones", [P, P])
        zero = sb("zero", [P, 1])
        wf_raw = sb("wf_raw", [P, KD * FOX_H])
        wf_hi = sb("wf_hi", [P, (KD - 1) * FOX_H + P], F32R)
        wf_lo = sb("wf_lo", [P, (KD - 1) * FOX_H + P], F32R)
        wa_raw = sb("wa_raw", [P, KD * GLA_RANK])
        wa_hi = sb("wa_hi", [P, (KD - 1) * GLA_RANK + P], F32R)
        wa_lo = sb("wa_lo", [P, (KD - 1) * GLA_RANK + P], F32R)
        b_forget = sb("b_forget", [FOX_H, 1])
        gate1 = sb("gate1", [P, 2, D])
        mod_col = sb("mod_col", [P, 2, 16])
        mod_bias = sb("mod_bias", [P, 2, 16])
        c_col = sb("c_col", [P, KD])
        conv = sb("conv", [P, sum(KF2), 4])
        tmp = sb("tmp", [P, 512])
        small = sb("small", [P, 148])
        row_max, neg_max, row_sum, row_inv = (small[:, 4 * i:4 * i + 4] for i in range(4))
        ln_sum = small[:, 16:24].rearrange("p (t h) -> p t h", h=2)
        ln_nmean, ln_ssq = small[:, 24:28], small[:, 28:32]
        gn_mv = small[:, 36:68].rearrange("p (t h c) -> p t h c", h=RET_H, c=2)
        gn_stats = small[:, 68:92].rearrange("p (t c) -> p t c", c=6)
        var, newton, rstd = small[:, 92:108], small[:, 108:124], small[:, 124:140]
        gla_ssq = small[:, 140:148].rearrange("p (a h) -> p a h", h=GLA_H)

        PS = ctx.enter_context(nc.psum_tensor("PS", [P, 8, HALF], F32))

        def stage(*tensors):
            with ExitStack() as own:
                return [own.enter_context(nc.sbuf_tensor(n, s, d)) for n, s, d in tensors]

        P_f, qT, kT, v_fox, PT, mix_hi, mix_lo, rq, rk, rv, cneg, gn_g, decay = stage(
            ("P_f", [P, PACKED], F32), ("qT", [P, 4, S], F32), ("kT", [P, 4, S], F32),
            ("v_fox", [P, NT, 512], F32), ("PT", [P, 4, S], F32), ("mix_hi", [P, 4, S], F32R), ("mix_lo", [P, 4, S], F32R),
            ("rq", [P, NT, 512], F32), ("rk", [P, NT, 512], F32), ("rv", [P, NT, 512], F32),
            ("cneg", [P, 2, S], F32), ("gn_g", [P, RET_H * RET_D], F32),
            ("decay", [P, RET_H, S], F32))
        rg = v_fox
        inner = (PT[:, :, :].rearrange("p a b -> p (a b)"), P_f)
        ln_p, hid_hi, hid_lo, mod_raw, mod_acc, relu_t = stage(
            ("ln_p", [P, 2, D], F32), ("hid_hi", [P, KF, S], F32R), ("hid_lo", [P, KF, S], F32R),
            ("mod_raw", [P, MOD_SLOTS, 512], F32), ("mod_acc", [P, 512], F32), ("relu_t", [P, 2, S], F32))
        (gq, gk, la, gv, go, state, bT, e_pos, e_neg, att, e_end, sil, alrT, w_a2, norm_g) = stage(
            ("gq", [P, GLA_H, S], F32), ("gk", [P, GLA_H, S], F32), ("la", [P, NT, 512], F32),
            ("gv", [P, NT, D], F32), ("go", [P, NT, D], F32), ("state", [P, 2, GLA_H, GLA_DV], F32),
            ("bT", [P, S], F32), ("e_pos", [P, S], F32), ("e_neg", [P, S], F32),
            ("att", [P, GLA_H, GLA_C], F32), ("e_end", [P, GLA_H, NC], F32),
            ("sil", [P, 2, 512], F32), ("alrT", [GLA_RANK + 1, S], F32),
            ("w_a2", [GLA_RANK + 1, 512], F32), ("norm_g", [P, GLA_DV], F32))
        kdT = go[:, 0:2, :].rearrange("p a (b s) -> p (a b) s", s=S)
        ln_p2, hid2_hi, hid2_lo, u_pad, u_conv = stage(
            ("ln_p2", [P, 2, D], F32), ("hid2_hi", [P, KF2[0], S], F32R), ("hid2_lo", [P, KF2[0], S], F32R),
            ("u_pad", [P, 2 + S], F32), ("u_conv", [P, 2, S], F32))

        raw_in = [sem(f"raw_in{i}") for i in range(RING)]
        w_hi_done = sem("w_hi_done")
        w_ready = sem("w_ready")
        w_begun = sem("w_begun")
        full_a = [sem(f"full_a{i}") for i in range(8)]
        full_v = [sem(f"full_v{i}") for i in range(8)]
        drained = [sem(f"drained{i}") for i in range(8)]
        a_did = sem("a_did")
        v_did = sem("v_did")
        v_saw, pe_saw = sem("v_saw"), sem("pe_saw")
        const_in = sem("const_in")
        const_ok = sem("const_ok")
        x_in = sem("x_in")
        x_ready = sem("x_ready")
        hi_ok = sem("hi_ok")
        lay_in = sem("lay_in")
        wf_ok = sem("wf_ok")
        f_log = sem("f_log")
        c_ok = sem("c_ok")
        c_out = sem("c_out")
        cb_in = [sem(f"cb_in{i}") for i in range(2)]
        max_ok = sem("max_ok")
        exp_ok = sem("exp_ok")
        p_ok = sem("p_ok")
        ret_raw = sem("ret_raw")
        rot_ok = sem("rot_ok")
        inner_ok = sem("inner_ok")
        ret_ok = sem("ret_ok")
        o_ok = sem("o_ok")
        ln_in = sem("ln_in")
        y_ok = sem("y_ok")
        sq_ok = sem("sq_ok")
        relu_ok = sem("relu_ok")
        hid_ok = sem("hid_ok")
        mod_in = [sem(f"mod_in{i}") for i in range(MOD_SLOTS)]
        mod_used = sem("mod_used")
        modp_in = sem("modp_in")
        cs_ok = sem("cs_ok")
        wa_ok = sem("wa_ok")
        g_in = sem("g_in")
        one_ok = sem("one_ok")
        la_log = sem("la_log")
        la_ok = sem("la_ok")
        b_ok = sem("b_ok")
        e_ok = sem("e_ok")
        qk_ok = sem("qk_ok")
        att_ok = sem("att_ok")
        st_ok = sem("st_ok")
        gsq_ok = sem("gsq_ok")
        sil_ok = sem("sil_ok")
        sil_used = sem("sil_used")
        go_ok = sem("go_ok")
        mx_ok = sem("mx_ok")
        u_ok = sem("u_ok")
        cv_ok = sem("cv_ok")
        su_ok = sem("su_ok")
        out_done = sem("out_done")

        block = ctx.enter_context(nc.Block())

        def fox_bank(h, job):
            return 4 + (7 * h + job) % 3

        BESIDE = (("q", 0, 2), ("q", 2, 2), ("k", 0, 1), ("k", 1, 1), ("k", 2, 1), ("k", 3, 1), ("v", 0, 2),
                  ("v", 2, 2))
        RET_BANKS = ((4, (0,)), (5, (1, 3)), (6, (2,)))

        def four(bank):
            return PS[:, bank, :].rearrange("p (j c) -> p j c", c=P)

        def chunk(tc):
            return slice(tc * P, (tc + 1) * P)

        def half(g):
            return slice(g * HALF, (g + 1) * HALF)

        def over(ap, count):
            return ap.unsqueeze(1).broadcast_to([ap.shape[0], count, ap.shape[1]])

        @block.sync
        def _(sp):
            n = Steps("sp", per_turn)
            for u in range(RING):
                sp.dma_start(raw[:, u, :], t["stream"][u]).then_inc(raw_in[u], 16)
            turns, rest = divmod(n_units - RING, RING)

            def refill(at, u):
                sp.wait_ge(w_ready, n.up(w_ready))
                sp.dma_start(raw[:, u, :], t["stream"][at]).then_inc(raw_in[u], 16)

            with n.loop(sp, turns) as i:
                for u in range(RING):
                    refill(sp.snap(i * RING + (RING + u)), u)
            for u in range(rest):
                refill(RING + turns * RING + u, u)
            n.skip(x_ready, NT * (2 + 2 * LAYERS))
            for tc in range(NT):
                sp.wait_ge(x_ready, n.up(x_ready))
                sp.dma_start(t["out"][tc], x[:, tc, :]).then_inc(out_done, 16)
            sp.wait_ge(out_done, 16 * NT)

        @block.gpsimd
        def _(pool):
            n = Steps("pool", per_turn)
            pool.wait_ge(const_ok, 1)
            n.skip(w_begun, 1)

            def cut(u, again=True):
                pool.wait_ge(raw_in[u], n.up(raw_in[u], 16))
                if again:
                    pool.wait_ge(w_begun, n.up(w_begun))
                nc.gpsimd.tensor_tensor(w_hi[:, u, :], raw[:, u, :], zero[:, 0:1].broadcast_to([P, UNIT]),
                                        ALU.add).then_inc(w_hi_done, 1)
                pool.wait_ge(w_hi_done, n.up(w_hi_done))
                nc.gpsimd.tensor_tensor(w_lo[:, u, :], raw[:, u, :], w_hi[:, u, :].bitcast(F32),
                                        ALU.subtract).then_inc(w_ready, 1)

            for u in range(RING):
                cut(u, again=False)
            turns, rest = divmod(n_units - RING, RING)
            with n.loop(pool, turns):
                for u in range(RING):
                    cut(u)
            for u in range(rest):
                cut(u)

        @block.tensor
        def _(pe):
            n = Steps("pe", per_turn)
            units = [0]
            mm, turn = nc.tensor.matmul, nc.tensor.transpose

            def take(b):
                pe.wait_ge(drained[b], n.up(drained[b]))

            def after(b):
                pe.wait_ge(drained[b], n.at(drained[b], 1))

            def next_unit():
                pe.wait_ge(w_ready, n.up(w_ready))
                units[0] += 1
                return (units[0] - 1) % RING

            def across(bank):
                take(bank)
                s = next_unit()
                out = PS[:, bank, :]
                for k in range(KD):
                    hi, lo = (w[:, s, chunk(k)] for w in (w_hi, w_lo))
                    ins = mm(out, hi, xT_hi[:, k, :], start=k == 0, stop=False)
                    if k == 0:
                        ins.then_inc(w_begun, 1)
                    mm(out, hi, xT_lo[:, k, :], start=False, stop=False)
                    last = mm(out, lo, xT_hi[:, k, :], start=False, stop=k == KD - 1)
                return last

            def of_x(k, tc):
                return xT_hi[:, k, chunk(tc)], xT_lo[:, k, chunk(tc)]

            def of_mixed(k, tc):
                return (mix_hi[:, k, chunk(tc)], mix_lo[:, k, chunk(tc)]) if k < 4 else of_x(k, tc)

            def of_hidden(k, tc):
                return hid_hi[:, k, chunk(tc)], hid_lo[:, k, chunk(tc)]

            def of_hidden_2(k, tc):
                return hid2_hi[:, k, chunk(tc)], hid2_lo[:, k, chunk(tc)]

            def down_chunk(a, k0, bank, tc, s, begins, first, last):
                out = PS[:, bank, :]
                for kk in range(2):
                    hi, lo = (w[:, s, half(kk)] for w in (w_hi, w_lo))
                    a_hi, a_lo = a(k0 + kk, tc)
                    ins = mm(out, a_hi, hi, start=first and kk == 0, stop=False)
                    if begins and kk == 0:
                        ins.then_inc(w_begun, 1)
                    mm(out, a_hi, lo, start=False, stop=False)
                    ins = mm(out, a_lo, hi, start=False, stop=last and kk == 1)
                return ins

            def down(a, bank0, full, count, of=None, at=0, stagger=False, before=lambda u: None):
                of = of or count
                for u in range(at, at + count - (RING if stagger else 0)):
                    before(u)
                    if u == 0:
                        for tc in range(NT):
                            take(bank0 + tc)
                    s = next_unit()
                    for tc in range(NT):
                        ins = down_chunk(a, 2 * u, bank0 + tc, tc, s, tc == 0, u == 0, u == of - 1)
                        if u == of - 1:
                            ins.then_inc(full[bank0 + tc], 1)
                if stagger:
                    slots = {}
                    for tc in range(NT):
                        for u in range(of - RING, of):
                            if tc == 0:
                                before(u)
                                slots[u] = next_unit()
                            if u == 0:
                                take(bank0 + tc)
                            begins = (tc == 0) if u == of - RING else (tc == NT - 1)
                            ins = down_chunk(a, 2 * u, bank0 + tc, tc, slots[u], begins,
                                             u == 0, u == of - 1)
                        ins.then_inc(full[bank0 + tc], 1)

            def blocks_to_bank(b, blocks):
                take(b)
                for j, src in enumerate(blocks):
                    last = turn(PS[:, b, chunk(j)], src, ident[:, :])
                return last

            def to_xT(src, ready):
                for tc in range(NT):
                    pe.wait_ge(ready, n.up(ready))
                    for g in range(2):
                        b = 4 + 2 * (tc % 2) + g
                        blocks_to_bank(b, [src[:, tc, chunk(4 * g + j)] for j in range(4)]).then_inc(full_a[b], 1)
                for b in range(4, 8):
                    after(b)

            def to_xT_modulated():
                pe.wait_ge(x_ready, n.up(x_ready, NT))
                for k in range(KD):
                    b = 4 + k % 4
                    blocks_to_bank(b, [x[:, tc, chunk(k)] for tc in range(NT)]).then_inc(full_a[b], 1)
                pe.wait_ge(mx_ok, n.up(mx_ok, KD))

            def narrow(bank, hi, lo, m):
                take(bank)
                for k in range(KD):
                    c = slice(k * m, k * m + P)
                    mm(PS[:, bank, :], hi[:, c], xT_hi[:, k, :], start=k == 0, stop=False)
                    mm(PS[:, bank, :], hi[:, c], xT_lo[:, k, :], start=False, stop=False)
                    last = mm(PS[:, bank, :], lo[:, c], xT_hi[:, k, :], start=False, stop=k == KD - 1)
                return last

            def fox_scores(h):
                r, c = FOX_D * (h % 2), h // 2
                for i in range(NT):
                    b, w = fox_bank(h, i), P * (i + 1)
                    take(b)
                    mm(PS[:, b, 0:w], qT[r:r + FOX_D, c, chunk(i)], kT[r:r + FOX_D, c, 0:w],
                       start=True, stop=False)
                    mm(PS[:, b, chunk(i)], ident_b[:, :], mask_b[:, :], start=False,
                       stop=True).then_inc(full_v[b], 1)

            def fox_transposes(h):
                for job, rows in enumerate(((0, 1), (2,), (3,))):
                    pe.wait_ge(p_ok, n.up(p_ok, len(rows)))
                    blocks = [P_f[:, ROW_OFF[i] + j * P:ROW_OFF[i] + (j + 1) * P]
                              for i in rows for j in range(i + 1)]
                    b = fox_bank(h, NT + job)
                    blocks_to_bank(b, blocks).then_inc((full_v if job == 1 else full_a)[b], 1)

            def fox_values(h):
                r = FOX_D * (h % 2)
                if h % 2 == 0:
                    take(7)
                for j in range(NT):
                    last = mm(PS[r:r + FOX_D, 7, j * P:S], v_fox[:, j, h * FOX_D:(h + 1) * FOX_D],
                              PT[:, j, j * P:S], start=j == 0, stop=j == NT - 1)
                if h % 2:
                    last.then_inc(full_v[7], 1)

            def ret_scores(h):
                for b, blocks in RET_BANKS:
                    take(b)
                    at = 0
                    for j in blocks:
                        w = S - j * P
                        last = mm(PS[:, b, at:at + w], kT[:, h, chunk(j)], qT[:, h, j * P:S],
                                  start=True, stop=True)
                        at += w
                    last.then_inc(full_v[b], 1)

            def ret_values(h):
                take(7)
                pe.wait_ge(inner_ok, n.up(inner_ok, NT))
                for i in range(NT):
                    for j in range(i + 1):
                        o = COL_OFF[j] + (i - j) * P
                        last = mm(PS[:, 7, chunk(i)], inner[h % 2][:, o:o + P], rv[:, j, chunk(h)],
                                  start=j == 0, stop=j == i)
                last.then_inc(full_a[7], 1)

            def mod_reduce(g):
                pe.wait_ge(mod_used, n.up(mod_used, KD))
                take(4)
                if g < 4:
                    for j in range(4):
                        last = mm(PS[:, 4, j:j + 1], mod_acc[:, chunk(j)], ones[:, 0:1], start=True, stop=True)
                else:
                    last = mm(PS[:, 4, :], ones[:, :], mod_acc[:, :], start=True, stop=True)
                last.then_inc(full_v[4], 1)

            pe.wait_ge(const_in, 16 * 4)
            pe.wait_ge(const_ok, 1)
            n.skip(mod_used, MOD_SLOTS)
            with n.loop(pe, LAYERS):
                to_xT(x, x_ready)
                pe.wait_ge(wf_ok, n.up(wf_ok))
                narrow(0, wf_hi, wf_lo, FOX_H).then_inc(full_a[0], 1)
                for u in range(8):
                    b = 4 + u % 4
                    across(b).then_inc((full_a if u < 4 else full_v)[b], 1)
                down(of_x, 0, full_a, 4)
                for b in range(4, 8):
                    after(b)
                fox_scores(0)
                for h in range(FOX_H):
                    down(of_x, 0, full_a, BESIDE[h][2], of=4, at=BESIDE[h][1])
                    fox_transposes(h)
                    if h + 1 < FOX_H:
                        fox_scores(h + 1)
                    else:
                        for job in range(3):
                            after(fox_bank(h, NT + job))
                    fox_values(h)
                for src, full in ((rq, full_v), (rk, full_a)):
                    pe.wait_ge(rot_ok, n.up(rot_ok, NT))
                    for h in range(RET_H):
                        b = 4 + h % 3
                        blocks_to_bank(b, [src[:, tc, chunk(h)] for tc in range(NT)]).then_inc(full[b], 1)
                for b in (4, 5, 6):
                    after(b)
                ret_scores(0)
                for h in range(RET_H):
                    down(of_x, 0, full_a, 1, of=4, at=h)
                    if h + 1 < RET_H:
                        ret_scores(h + 1)
                    ret_values(h)
                down(of_mixed, 0, full_v, 2, of=4)
                for tc in range(NT):
                    pe.wait_ge(ret_ok, n.up(ret_ok))
                    b = 4 + tc
                    blocks_to_bank(b, [rq[:, tc, chunk(h)] for h in range(RET_H)]).then_inc(full_a[b], 1)
                for b in range(4, 8):
                    after(b)
                down(of_mixed, 0, full_v, 2, of=4, at=2)
                down(of_mixed, 4, full_v, 4, stagger=True)
                to_xT(x, x_ready)
                for part in range(2):
                    pe.sem_inc(pe_saw, 1)
                    with n.loop(pe, KF // RING):
                        for u in range(RING):
                            b = 4 + u % 2
                            across(b).then_inc(full_a[b], 1)

                    def before_down(u):
                        pe.wait_ge(hid_ok, n.up(hid_ok, 2))
                        if u in (2, 4, 6):
                            mod_reduce(3 * part + u // 2 - 1)

                    down(of_hidden, 0, full_v, KF // 2, before=before_down)
                    down(of_hidden, 4, full_v, KF // 2, stagger=part == 1)

            to_xT_modulated()
            pe.wait_ge(wa_ok, 1)
            narrow(0, wa_hi, wa_lo, GLA_RANK).then_inc(full_v[0], 1)
            for u in range(8):
                b = 4 + u % 4
                across(b).then_inc((full_a if u < 4 else full_v)[b], 1)
            after(0)
            pe.wait_ge(g_in, 16 * 3)
            for tc in range(NT):
                take(tc)
                mm(PS[:, tc, :], alrT[:, chunk(tc)], w_a2[:, :], start=True, stop=True).then_inc(full_a[tc], 1)
            down(of_x, 0, full_a, 4)
            pe.wait_ge(la_ok, n.up(la_ok, NT))

            def gate_sums(h):
                b = 4 + h % 2
                take(b)
                for tc in range(NT):
                    last = mm(PS[:, b, chunk(tc)], la[:, tc, chunk(h)], masks[:, P:2 * P], start=True, stop=True)
                last.then_inc(full_v[b], 1)

            down(of_x, 0, full_a, 4, before=gate_sums)
            for h in range(GLA_H):
                pe.wait_ge(qk_ok, n.up(qk_ok))
                b = 6 + h % 2
                blocks_to_bank(b, [kdT[:, h, chunk(tc)] for tc in range(NT)]).then_inc(full_a[b], 1)
            for b in (0, 1, 2, 3, 6, 7):
                after(b)
            for c in range(NC):
                tc, r = c // 2, GLA_C * (c % 2)
                rows, tok = slice(r, r + GLA_C), slice(c * GLA_C, (c + 1) * GLA_C)
                take(4)
                for h in range(GLA_H):
                    last = mm(PS[rows, 4, h * GLA_C:(h + 1) * GLA_C], gk[:, h, tok], gq[:, h, tok],
                              start=True, stop=True)
                last.then_inc(full_v[4], 1)
                if c < NC - 1:
                    for h in range(GLA_H):
                        b = 5 + h // 2
                        if h % 2 == 0:
                            take(b)
                        last = mm(PS[:, b, (h % 2) * GLA_DV:(h % 2 + 1) * GLA_DV], la[rows, tc, chunk(h)],
                                  gv[rows, tc, h * GLA_DV:(h + 1) * GLA_DV], start=True, stop=True)
                        if h % 2:
                            last.then_inc(full_v[b], 1)
                o_bank = 2 * (tc % 2)
                if c % 2 == 0:
                    take(o_bank)
                    take(o_bank + 1)
                pe.wait_ge(att_ok, n.up(att_ok))
                if c:
                    pe.wait_ge(st_ok, n.up(st_ok))
                for h in range(GLA_H):
                    out = PS[rows, o_bank + h // 2, (h % 2) * GLA_DV:(h % 2 + 1) * GLA_DV]
                    last = mm(out, att[rows, h, :], gv[rows, tc, h * GLA_DV:(h + 1) * GLA_DV],
                              start=True, stop=c == 0)
                    if c:
                        last = mm(out, gq[:, h, tok], state[:, c % 2, h, :], start=False, stop=True)
                    if c % 2 and h % 2:
                        last.then_inc(full_a[o_bank + h // 2], 1)
            down(of_x, 0, full_a, 4)
            down(of_x, 4, full_a, 4, stagger=True)
            to_xT(go, go_ok)
            down(of_x, 0, full_v, 4)
            down(of_x, 4, full_v, 4, stagger=True)
            to_xT_modulated()
            for part, kf in enumerate(KF2):
                with n.loop(pe, kf // 2):
                    for u in range(RING):
                        b = 4 + u
                        across(b).then_inc((full_v if u % 2 else full_a)[b], 1)
                down(of_hidden_2, 0, full_v, kf // 2,
                     before=lambda u: pe.wait_ge(hid_ok, n.up(hid_ok, 2)))
                down(of_hidden_2, 4, full_v, kf // 2, stagger=part == 1)

        @block.scalar
        def _(act):
            n = Steps("act", per_turn)
            run = nc.scalar.activation

            def own(ins):
                ins.then_inc(a_did, 1)
                act.wait_ge(a_did, n.up(a_did))

            def bank(b):
                act.wait_ge(full_a[b], n.up(full_a[b]))

            def hi_of_xT():
                for tc in range(NT):
                    for g in range(2):
                        b = 4 + 2 * (tc % 2) + g
                        bank(b)
                        run(xT_hi[:, 4 * g:4 * g + 4, chunk(tc)], four(b), ACT.Copy).then_inc(hi_ok, 1)

            def hi_modulated(sub):
                for k in range(KD):
                    b = 4 + k % 4
                    bank(b)
                    run(xT_hi[:, k, :], PS[:, b, :], ACT.Identity, scale=mod_col[:, sub, 8 + k:9 + k],
                        bias=mod_col[:, sub, k:k + 1]).then_inc(hi_ok, 1)

            def squares(junk):
                for tc in range(NT):
                    act.wait_ge(y_ok, n.up(y_ok))
                    run(junk, x[:, tc, :], ACT.Square, bias=ln_nmean[:, tc:tc + 1],
                        accum_out=ln_ssq[:, tc:tc + 1]).then_inc(sq_ok, 1)
                    act.wait_ge(sq_ok, n.up(sq_ok))

            def load_ln(g, b, dst):
                act.dma_start(dst[:, 0, :], g.broadcast_to([P, D])).then_inc(ln_in, 16)
                act.dma_start(dst[:, 1, :], b.broadcast_to([P, D])).then_inc(ln_in, 16)

            act.dma_start(x[:, :, :], t["x"]).then_inc(x_in, 16)
            for name, dst in (("ident", ident), ("masks", masks), ("cos", cos_t), ("sin", sin_t)):
                act.dma_start(dst[:], t[name]).then_inc(const_in, 16)
            for name, dst in (("c", c_col), ("mod_bias", mod_bias), ("gate_bias", gate1), ("conv", conv),
                              ("w_a", wa_raw)):
                act.dma_start(dst[:], t[name]).then_inc(modp_in, 16)
            act.wait_ge(modp_in, 16 * 5)
            run(c_col[:, :], c_col[:, :], ACT.Silu).then_inc(cs_ok, 1)
            n.skip(x_ready, NT)
            with n.loop(act, LAYERS) as layer:
                act.wait_ge(x_ready, n.at(x_ready))
                act.dma_start(wf_raw[:, :], t["w_forget"][layer]).then_inc(lay_in, 16)
                act.dma_start(b_forget[:, :], t["b_forget"][layer]).then_inc(lay_in, 16)
                act.dma_start(gn_g[:, :], t["gn_g"][layer].broadcast_to([P, RET_H * RET_D])).then_inc(lay_in, 16)
                act.dma_start(decay[:, :, :], t["decay"]).then_inc(lay_in, 16)
                hi_of_xT()
                act.wait_ge(lay_in, n.up(lay_in, 16 * 4))
                bank(0)
                fe = P_f[0:FOX_H, 0:S]
                own(run(fe, PS[0:FOX_H, 0, :], ACT.Abs, bias=b_forget[:, 0:1]))
                own(run(fe, fe, ACT.Exp, scale=-1.0))
                run(fe, fe, ACT.Ln, bias=1.0).then_inc(f_log, 1)
                for u in range(4):
                    b = 4 + u
                    bank(b)
                    run(qT[:, u, :], PS[:, b, :], ACT.Copy).then_inc(drained[b], 1)
                act.wait_ge(c_ok, n.up(c_ok))
                act.dma_start(t["c_scratch"], P_f[0:FOX_H, S:2 * S]).then_inc(c_out, 16)
                act.wait_ge(c_out, n.up(c_out, 16))

                def load_c(h):
                    act.dma_start(cneg[:, h % 2, :], t["c_scratch"][h:h + 1, :].broadcast_to([P, S])).then_inc(
                        cb_in[h % 2], 16)

                def projection_out(dst, function):
                    for b in range(4):
                        bank(b)
                        run(dst[:, b, :], PS[:, b, :], function).then_inc(drained[b], 1)
                    act.drain().then_inc(ret_raw, 1)

                load_c(0)
                load_c(1)
                for b in range(4):
                    bank(b)
                    run(v_fox[:, b, :], PS[:, b, :], ACT.Copy).then_inc(drained[b], 1)
                for h in range(FOX_H):
                    act.wait_ge(max_ok, n.up(max_ok))
                    if h + 2 < FOX_H:
                        load_c(h + 2)
                    for i in range(NT):
                        rows = P_f[:, ROW_OFF[i]:ROW_OFF[i] + P * (i + 1)]
                        run(rows, rows, ACT.Exp, bias=neg_max[:, i:i + 1], scale=FOX_SCALE,
                            accum_out=row_sum[:, i:i + 1]).then_inc(exp_ok, 1)
                    b = fox_bank(h, NT)
                    bank(b)
                    run(PT[:, 0, 0:P], PS[:, b, 0:P], ACT.Copy)
                    run(PT[:, 0:2, P:2 * P], four(b)[:, 1:3, :], ACT.Copy).then_inc(drained[b], 1)
                    b = fox_bank(h, NT + 2)
                    bank(b)
                    run(PT[:, :, 3 * P:], four(b), ACT.Copy).then_inc(drained[b], 1)
                    which, at, count = BESIDE[h]
                    if at + count == 4:
                        projection_out({"q": rq, "k": rk, "v": rv}[which], ACT.Copy)
                for h in range(RET_H):
                    b = 4 + h % 3
                    bank(b)
                    run(kT[:, h, :], PS[:, b, :], ACT.Copy).then_inc(drained[b], 1)
                for h in range(RET_H):
                    if h == RET_H - 1:
                        projection_out(rg, ACT.Silu)
                    bank(7)
                    run(rq[:, :, chunk(h)], four(7), ACT.Copy).then_inc(drained[7], 1)
                    act.drain().then_inc(o_ok, 1)
                for tc in range(NT):
                    b = 4 + tc
                    bank(b)
                    run(xT_hi[:, 4:8, chunk(tc)], four(b), ACT.Copy).then_inc(hi_ok, 1)
                load_ln(t["ln1_g"][layer], t["ln1_b"][layer], ln_p)
                squares(relu_t[:, :, :].rearrange("p a b -> p (a b)"))
                act.wait_ge(x_ready, n.up(x_ready, NT))
                load_ln(t["ln2_g"][layer], t["ln2_b"][layer], ln_p)
                hi_of_xT()
                def load_mod(number):
                    g, k = divmod(number, KD)
                    slot = number % MOD_SLOTS
                    act.wait_ge(mod_used, n.up(mod_used))
                    act.dma_start(mod_raw[:, slot, :], t["mod"][layer, g, k]).then_inc(mod_in[slot], 16)

                for number in range(MOD_SLOTS):
                    load_mod(number)
                for part in range(2):
                    with n.loop(act, KF // RING):
                        for u in range(RING):
                            b = 4 + u % 2
                            bank(b)
                            run(relu_t[:, u % 2, :], PS[:, b, :], ACT.Relu).then_inc(relu_ok, 1)
                    for number in range(3 * KD):
                        number += 3 * KD * part + MOD_SLOTS
                        if number < MOD_GROUPS * KD:
                            load_mod(number)
                squares(relu_t[:, :, :].rearrange("p a b -> p (a b)"))
                n.skip(x_ready, NT)

            act.wait_ge(x_ready, n.at(x_ready))
            act.dma_start(w_a2[0:GLA_RANK, :], t["w_a2"]).then_inc(g_in, 16)
            act.dma_start(w_a2[GLA_RANK:GLA_RANK + 1, :], t["b_a"]).then_inc(g_in, 16)
            act.dma_start(norm_g[:, :], t["norm_g"].broadcast_to([P, GLA_DV])).then_inc(g_in, 16)
            hi_modulated(0)
            for u in range(4):
                b = 4 + u
                bank(b)
                run(gq[:, u, :], PS[:, b, :], ACT.Copy, scale=GLA_DK ** -0.5).then_inc(drained[b], 1)
            for tc in range(NT):
                bank(tc)
                own(run(la[:, tc, :], PS[:, tc, :], ACT.Abs))
                own(run(la[:, tc, :], la[:, tc, :], ACT.Exp, scale=-1.0))
                run(la[:, tc, :], la[:, tc, :], ACT.Ln, bias=1.0).then_inc(la_log, 1)
            for tc in range(NT):
                bank(tc)
                run(gv[:, tc, half(0)], PS[:, tc, :], ACT.Copy).then_inc(drained[tc], 1)
            for h in range(GLA_H):
                act.wait_ge(b_ok, n.up(b_ok))
                run(e_pos[:, :], bT[:, :], ACT.Exp, scale=1 / GLA_TAU)
                run(e_neg[:, :], bT[:, :], ACT.Exp, scale=-1 / GLA_TAU)
                run(e_end[:, h, :], bT[:, :].rearrange("p (c s) -> p c s", s=GLA_C)[:, :, GLA_C - 1],
                    ACT.Exp, scale=1 / GLA_TAU)
                run(kdT[:, h, :], kdT[:, h, :], ACT.Exp, scale=1 / GLA_TAU).then_inc(e_ok, 1)
            for tc in range(NT):
                bank(tc)
                run(gv[:, tc, half(1)], PS[:, tc, :], ACT.Copy).then_inc(drained[tc], 1)
            for h in range(GLA_H):
                b = 6 + h % 2
                bank(b)
                run(la[:, :, chunk(h)], four(b), ACT.Copy).then_inc(drained[b], 1)
            for tc in range(NT):
                for h in range(GLA_H):
                    b = 2 * (tc % 2) + h // 2
                    if h % 2 == 0:
                        bank(b)
                    ins = run(sil[:, 0, 0:GLA_DV], PS[:, b, (h % 2) * GLA_DV:(h % 2 + 1) * GLA_DV],
                              ACT.Square, accum_out=gla_ssq[:, tc % 2, h:h + 1])
                    if h < GLA_H - 1:
                        own(ins)
                    else:
                        ins.then_inc(gsq_ok, 1)
            for g in range(2):
                for tc in range(NT):
                    b = 4 * g + tc
                    bank(b)
                    act.wait_ge(sil_used, n.up(sil_used))
                    run(sil[:, tc % 2, :], PS[:, b, :], ACT.Silu).then_inc(sil_ok, 1)
            hi_of_xT()
            load_ln(t["ln_g_2"][0:1, :], t["ln_b_2"][0:1, :], ln_p2)
            squares(u_conv[:, :, :].rearrange("p a b -> p (a b)"))
            act.wait_ge(x_ready, n.up(x_ready, NT))
            load_ln(t["ln_g_2"][1:2, :], t["ln_b_2"][1:2, :], ln_p2)
            hi_modulated(1)
            for part, kf in enumerate(KF2):
                with n.loop(act, kf // 2):
                    for u in range(2):
                        bank(4 + 2 * u)
                        run(u_pad[:, 2:2 + S], PS[:, 4 + 2 * u, :], ACT.Copy).then_inc(u_ok, 1)
                        act.wait_ge(cv_ok, n.up(cv_ok))
                        run(u_conv[:, 0, :], u_conv[:, 1, :], ACT.Silu).then_inc(su_ok, 1)
            squares(u_conv[:, :, :].rearrange("p a b -> p (a b)"))

        @block.vector
        def _(ve):
            n = Steps("ve", per_turn)
            v = nc.vector

            def own(ins):
                ins.then_inc(v_did, 1)
                ve.wait_ge(v_did, n.up(v_did))

            def fence():
                ve.drain().then_inc(v_did, 1)
                ve.wait_ge(v_did, n.up(v_did))

            def bank(b):
                ve.wait_ge(full_v[b], n.up(full_v[b]))

            def settled():
                ve.sem_inc(v_saw, 1)

            def lo_of_xT():
                for tc in range(NT):
                    for g in range(2):
                        b = 4 + 2 * (tc % 2) + g
                        cols = (slice(None), slice(4 * g, 4 * g + 4), chunk(tc))
                        ve.wait_ge(hi_ok, n.up(hi_ok))
                        v.tensor_tensor(xT_lo[cols], four(b), xT_hi[cols].bitcast(F32),
                                        ALU.subtract).then_inc(drained[b], 1)

            def modulated(sub):
                for k in range(KD):
                    b = 4 + k % 4
                    ve.wait_ge(hi_ok, n.up(hi_ok))
                    own(v.tensor_scalar(tmp[:, :], PS[:, b, :], mod_col[:, sub, 8 + k:9 + k],
                                        mod_col[:, sub, k:k + 1], ALU.mult, ALU.add))
                    ve.sem_inc(drained[b], 1)
                    v.tensor_tensor(xT_lo[:, k, :], tmp[:, :], xT_hi[:, k, :].bitcast(F32),
                                    ALU.subtract).then_inc(mx_ok, 1)
                    fence()

            def rsqrt_col(out, arg, by):
                own(v.tensor_scalar(by.bitcast(I32), arg.bitcast(I32), 1, None, ALU.logical_shift_right))
                own(v.tensor_scalar(out.bitcast(I32), by.bitcast(I32), -1.0, 1597463007.0, ALU.mult, ALU.add))
                own(v.tensor_scalar(arg, arg, -0.5, None, ALU.mult))
                for _ in range(3):
                    own(v.scalar_tensor_tensor(out=by, in0=out, scalar=arg, in1=out, op0=ALU.mult, op1=ALU.mult))
                    own(v.scalar_tensor_tensor(out=out, in0=by, scalar=1.5, in1=out, op0=ALU.add, op1=ALU.mult))

            def rsqrt(out, arg, by):
                own(v.tensor_scalar(by.bitcast(I32), arg.bitcast(I32), 1, None, ALU.logical_shift_right))
                own(v.tensor_scalar(out.bitcast(I32), by.bitcast(I32), -1.0, 1597463007.0, ALU.mult, ALU.add))
                for _ in range(3):
                    own(v.tensor_tensor(by, out, out, ALU.mult))
                    own(v.tensor_tensor(by, by, arg, ALU.mult))
                    own(v.tensor_scalar(by, by, -0.5, 1.5, ALU.mult, ALU.add))
                    own(v.tensor_tensor(out, out, by, ALU.mult))

            def add_to_x(tc, g, scale, gate=None, b=None, accumulate=False):
                b = 4 * g + tc if b is None else b
                bank(b)
                src = PS[:, b, :]
                if gate is not None:
                    own(v.tensor_tensor(tmp[:, :], src, gate[:, half(g)], ALU.mult))
                    src = tmp[:, :]
                out = x[:, tc, half(g)]
                v.scalar_tensor_tensor(out=out, in0=out, scalar=scale, in1=src, op0=ALU.mult, op1=ALU.add,
                                       accum_out=ln_sum[:, tc, g:g + 1] if accumulate else None).then_inc(
                    drained[b], 1)
                fence()

            def layer_norm(params, scale, gate=None):
                for tc in range(NT):
                    add_to_x(tc, 0, scale, gate, accumulate=True)
                ve.wait_ge(ln_in, n.up(ln_in, 32))

                def sums(tc):
                    add_to_x(tc, 1, scale, gate, accumulate=True)
                    v.tensor_scalar(ln_nmean[:, tc:tc + 1], ln_sum[:, tc, 0:1], ln_sum[:, tc, 1:2], -1.0 / D,
                                    ALU.add, ALU.mult).then_inc(y_ok, 1)
                    fence()

                def normalise(tc):
                    ve.wait_ge(sq_ok, n.up(sq_ok))
                    own(v.tensor_scalar(var[:, 0:1], ln_ssq[:, tc:tc + 1], 1.0 / D, EPS, ALU.mult, ALU.add))
                    rsqrt_col(rstd[:, 0:1], var[:, 0:1], newton[:, 0:1])
                    own(v.scalar_tensor_tensor(out=x[:, tc, :], in0=x[:, tc, :], scalar=ln_nmean[:, tc:tc + 1],
                                               in1=params[:, 0, :], op0=ALU.add, op1=ALU.mult))
                    v.scalar_tensor_tensor(out=x[:, tc, :], in0=x[:, tc, :], scalar=rstd[:, 0:1],
                                           in1=params[:, 1, :], op0=ALU.mult, op1=ALU.add).then_inc(x_ready, 1)
                    fence()

                for tc in range(NT):
                    sums(tc)
                    if tc:
                        normalise(tc - 1)
                normalise(NT - 1)

            own(v.memset(zero[:, :], 0.0))
            own(v.memset(ones[:, :], 1.0))
            for w in (wf_hi, wf_lo, wa_hi, wa_lo):
                own(v.memset(w[:, :].bitcast(F32), 0.0))
            ve.wait_ge(const_in, 16 * 4)
            own(v.tensor_copy(ident_b[:, :], ident[:, :]))
            v.tensor_copy(mask_b[:, :], masks[:, 0:P]).then_inc(const_ok, 1)
            for b in range(8):
                ve.drain().then_inc(drained[b], 1)
            ve.drain().then_inc(mod_used, MOD_SLOTS)
            ve.drain().then_inc(sil_used, 2)
            ve.wait_ge(modp_in, 16 * 5)
            own(v.tensor_copy(wa_hi[:, 0:KD * GLA_RANK], wa_raw[:, :]))
            v.tensor_tensor(wa_lo[:, 0:KD * GLA_RANK], wa_raw[:, :], wa_hi[:, 0:KD * GLA_RANK].bitcast(F32),
                            ALU.subtract).then_inc(wa_ok, 1)
            ve.wait_ge(cs_ok, 1)
            ve.wait_ge(x_in, 16)
            ve.drain().then_inc(x_ready, NT)
            with n.loop(ve, LAYERS) as layer:
                ve.wait_ge(lay_in, n.up(lay_in, 16 * 4))
                own(v.tensor_copy(wf_hi[:, 0:KD * FOX_H], wf_raw[:, :]))
                v.tensor_tensor(wf_lo[:, 0:KD * FOX_H], wf_raw[:, :], wf_hi[:, 0:KD * FOX_H].bitcast(F32),
                                ALU.subtract).then_inc(wf_ok, 1)
                lo_of_xT()
                ve.wait_ge(f_log, n.up(f_log))
                fe, fm = P_f[0:FOX_H, 0:S], P_f[0:FOX_H, S:2 * S]
                own(v.tensor_scalar(fm, PS[0:FOX_H, 0, :], b_forget[:, 0:1], 0.0, ALU.add, ALU.min))
                ve.sem_inc(drained[0], 1)
                own(v.tensor_tensor(fm, fm, fe, ALU.subtract))
                own(v.tensor_tensor_scan(fe, ones[0:FOX_H, 0:1].broadcast_to([FOX_H, S]), fm, 0.0,
                                         ALU.mult, ALU.add))
                v.tensor_scalar(fm, fe, -1.0 / FOX_SCALE, None, ALU.mult).then_inc(c_ok, 1)
                for u in range(4):
                    b = 4 + u
                    bank(b)
                    v.tensor_copy(kT[:, u, :], PS[:, b, :]).then_inc(drained[b], 1)

                def pair_out(c):
                    bank(7)
                    own(v.tensor_copy(mix_hi[:, c, :], PS[:, 7, :]))
                    v.tensor_tensor(mix_lo[:, c, :], PS[:, 7, :], mix_hi[:, c, :].bitcast(F32),
                                    ALU.subtract).then_inc(drained[7], 1)

                def rotate(src, chunks):
                    for tc in chunks:
                        s3 = src[:, tc, :].rearrange("p (h e) -> p h e", e=RET_D)
                        t3 = tmp[:, :].rearrange("p (h e) -> p h e", e=RET_D)
                        e = RET_D // 2
                        own(v.tensor_tensor(t3[:, :, 0:e], s3[:, :, e:], over(sin_t[:, tc, 0, :], RET_H), ALU.mult))
                        own(v.tensor_tensor(t3[:, :, e:], s3[:, :, 0:e], over(sin_t[:, tc, 1, :], RET_H), ALU.mult))
                        own(v.tensor_tensor(src[:, tc, :].rearrange("p (h e) -> p h e", e=e),
                                            src[:, tc, :].rearrange("p (h e) -> p h e", e=e),
                                            over(cos_t[:, tc, :], 2 * RET_H), ALU.mult))
                        v.tensor_tensor(src[:, tc, :], src[:, tc, :], tmp[:, :], ALU.add).then_inc(rot_ok, 1)
                        fence()

                for h in range(FOX_H):
                    ve.wait_ge(cb_in[h % 2], n.up(cb_in[h % 2], 16))
                    for i in range(NT):
                        b, w = fox_bank(h, i), P * (i + 1)
                        bank(b)
                        settled()
                        v.tensor_tensor_reduce(out=P_f[:, ROW_OFF[i]:ROW_OFF[i] + w], in0=PS[:, b, 0:w],
                                               in1=cneg[:, h % 2, 0:w], scale=1.0, scalar=-3.0e38, op0=ALU.add,
                                               op1=ALU.max, accum_out=row_max[:, i:i + 1]).then_inc(drained[b], 1)
                    fence()
                    v.tensor_scalar(neg_max, row_max, -FOX_SCALE, None, ALU.mult).then_inc(max_ok, 1)
                    ve.wait_ge(exp_ok, n.up(exp_ok, NT))
                    own(v.reciprocal(row_inv, row_sum))
                    for i in range(NT):
                        rows = P_f[:, ROW_OFF[i]:ROW_OFF[i] + P * (i + 1)]
                        v.tensor_scalar(rows, rows, row_inv[:, i:i + 1], None, ALU.mult).then_inc(p_ok, 1)
                    if h and h % 2 == 0:
                        pair_out(h // 2 - 1)
                    b = fox_bank(h, NT + 1)
                    bank(b)
                    v.tensor_copy(PT[:, 0:3, 2 * P:3 * P], four(b)[:, 0:3, :]).then_inc(drained[b], 1)
                    if h in (2, 6):
                        ve.wait_ge(ret_raw, n.up(ret_raw))
                    if 2 <= h < 6:
                        rotate(rq, (h - 2,))
                    if h >= 6:
                        rotate(rk, (2 * h - 12, 2 * h - 11))
                pair_out(FOX_H // 2 - 1)
                for h in range(RET_H):
                    b = 4 + h % 3
                    bank(b)
                    v.tensor_copy(qT[:, h, :], PS[:, b, :]).then_inc(drained[b], 1)

                def decayed(h):
                    for b, blocks in RET_BANKS:
                        bank(b)
                        at = 0
                        for j in blocks:
                            w = S - j * P
                            v.tensor_tensor(inner[h % 2][:, COL_OFF[j]:COL_OFF[j] + w], PS[:, b, at:at + w],
                                            decay[:, h, 0:w], ALU.mult).then_inc(inner_ok, 1)
                            at += w
                        ve.drain().then_inc(drained[b], 1)

                def group_stats(h):
                    ve.wait_ge(o_ok, n.up(o_ok))
                    settled()
                    for tc in range(NT):
                        v.bn_stats(gn_stats[:, tc, :], rq[:, tc, chunk(h)])
                    fence()
                    settled()
                    for tc in range(NT):
                        v.bn_aggr(gn_mv[:, tc, h, :], gn_stats[:, tc, :])
                    fence()

                decayed(0)
                for h in range(RET_H):
                    if h + 1 < RET_H:
                        decayed(h + 1)
                    else:
                        ve.wait_ge(ret_raw, n.up(ret_raw, 2))
                        own(v.tensor_tensor(rg[:, :, :], rg[:, :, :], over(gn_g[:, :], NT), ALU.mult))
                    group_stats(h)
                own(v.tensor_scalar(var.rearrange("p (t h) -> p t h", h=RET_H), gn_mv[:, :, :, 1], EPS, None,
                                    ALU.add))
                rsqrt(rstd, var, newton)
                for tc in range(NT):
                    for h in range(RET_H):
                        v.tensor_scalar(rq[:, tc, chunk(h)], rq[:, tc, chunk(h)], gn_mv[:, tc, h, 0:1],
                                        rstd[:, 4 * tc + h:4 * tc + h + 1], ALU.subtract, ALU.mult)
                    fence()
                    v.tensor_tensor(rq[:, tc, :], rq[:, tc, :], rg[:, tc, :], ALU.mult).then_inc(ret_ok, 1)
                for tc in range(NT):
                    b = 4 + tc
                    ve.wait_ge(hi_ok, n.up(hi_ok))
                    v.tensor_tensor(xT_lo[:, 4:8, chunk(tc)], four(b), xT_hi[:, 4:8, chunk(tc)].bitcast(F32),
                                    ALU.subtract).then_inc(drained[b], 1)
                layer_norm(ln_p, ALPHA_1)
                lo_of_xT()
                for part in range(2):
                    settled()
                    with n.loop(ve, KF // RING) as i:
                        for u in range(RING):
                            b, dst = 4 + u % 2, bass.ds(i * RING + u, 1)
                            ve.wait_ge(relu_ok, n.up(relu_ok))
                            own(v.tensor_tensor(tmp[:, :], PS[:, b, :], relu_t[:, u % 2, :], ALU.mult))
                            ve.sem_inc(drained[b], 1)
                            own(v.tensor_copy(hid_hi[:, dst, :], tmp[:, :].unsqueeze(1)))
                            v.tensor_tensor(hid_lo[:, dst, :], tmp[:, :].unsqueeze(1),
                                            hid_hi[:, dst, :].bitcast(F32), ALU.subtract).then_inc(hid_ok, 1)
                            fence()
                    for g3 in range(3):
                        g = 3 * part + g3
                        for k in range(KD):
                            slot = (g * KD + k) % MOD_SLOTS
                            ve.wait_ge(mod_in[slot], n.up(mod_in[slot], 16))
                            if k == 0:
                                v.tensor_scalar(mod_acc[:, :], mod_raw[:, slot, :], c_col[:, 0:1], None,
                                                ALU.mult).then_inc(mod_used, 1)
                            else:
                                v.scalar_tensor_tensor(out=mod_acc[:, :], in0=mod_raw[:, slot, :],
                                                       scalar=c_col[:, k:k + 1], in1=mod_acc[:, :], op0=ALU.mult,
                                                       op1=ALU.add).then_inc(mod_used, 1)
                            fence()
                        bank(4)
                        if g < 4:
                            out = mod_col[:, bass.ds(layer, 1), 4 * g:4 * g + 4]
                            v.scalar_tensor_tensor(out=out, in0=PS[:, 4, 0:4].unsqueeze(1),
                                                   scalar=float(g >= 2),
                                                   in1=mod_bias[:, bass.ds(layer, 1), 4 * g:4 * g + 4],
                                                   op0=ALU.add, op1=ALU.add).then_inc(drained[4], 1)
                        else:
                            out = gate1[:, bass.ds(layer, 1), half(g - 4)]
                            v.scalar_tensor_tensor(out=out, in0=PS[:, 4, :].unsqueeze(1), scalar=1.0, in1=out,
                                                   op0=ALU.add, op1=ALU.add).then_inc(drained[4], 1)
                    if part == 0:
                        for g in range(2):
                            for tc in range(NT):
                                add_to_x(tc, g, ALPHA_1)
                layer_norm(ln_p, 1.0)

            v.memset(alrT[:, :], 1.0).then_inc(one_ok, 1)
            ve.wait_ge(one_ok, 1)
            modulated(0)
            bank(0)
            v.tensor_copy(alrT[0:GLA_RANK, :], PS[0:GLA_RANK, 0, :]).then_inc(drained[0], 1)
            for u in range(4):
                b = 4 + u
                bank(b)
                v.tensor_copy(gk[:, u, :], PS[:, b, :]).then_inc(drained[b], 1)
            for tc in range(NT):
                ve.wait_ge(la_log, n.up(la_log))
                own(v.scalar_tensor_tensor(out=la[:, tc, :], in0=PS[:, tc, :], scalar=0.0, in1=la[:, tc, :],
                                           op0=ALU.min, op1=ALU.subtract))
                ve.sem_inc(drained[tc], 1)
                ve.drain().then_inc(la_ok, 1)
            for h in range(GLA_H):
                b = 4 + h % 2
                b3 = bT[:, :].rearrange("p (c s) -> p c s", s=GLA_C)
                bank(b)
                own(v.tensor_copy(bT[:, :], PS[:, b, :]))
                ve.sem_inc(drained[b], 1)
                v.tensor_tensor(kdT[:, h, :].rearrange("p (c s) -> p c s", s=GLA_C),
                                b3[:, :, GLA_C - 1:GLA_C].broadcast_to([P, NC, GLA_C]), b3,
                                ALU.subtract).then_inc(b_ok, 1)
                ve.wait_ge(e_ok, n.up(e_ok))
                v.tensor_tensor(gq[:, h, :], gq[:, h, :], e_pos[:, :], ALU.mult)
                own(v.tensor_tensor(kdT[:, h, :], kdT[:, h, :], gk[:, h, :], ALU.mult))
                v.tensor_tensor(gk[:, h, :], gk[:, h, :], e_neg[:, :], ALU.mult).then_inc(qk_ok, 1)
            ve.wait_ge(g_in, 16 * 3)

            def gla_out(tc):
                ve.wait_ge(gsq_ok, n.up(gsq_ok))
                cols = slice(0, GLA_H)
                own(v.tensor_scalar(var[:, cols], gla_ssq[:, tc % 2, :], 1.0 / GLA_DV, EPS, ALU.mult, ALU.add))
                rsqrt(rstd[:, cols], var[:, cols], newton[:, cols])
                for h in range(GLA_H):
                    b, cols = 2 * (tc % 2) + h // 2, slice((h % 2) * GLA_DV, (h % 2 + 1) * GLA_DV)
                    ins = v.scalar_tensor_tensor(out=go[:, tc, h * GLA_DV:(h + 1) * GLA_DV], in0=PS[:, b, cols],
                                                 scalar=rstd[:, h:h + 1], in1=norm_g[:, :], op0=ALU.mult,
                                                 op1=ALU.mult)
                    if h % 2:
                        ins.then_inc(drained[b], 1)
                fence()

            for c in range(NC):
                r = GLA_C * (c % 2)
                rows = slice(r, r + GLA_C)
                bank(4)
                v.tensor_tensor(att[rows, :, :], PS[rows, 4, 0:GLA_H * GLA_C].rearrange("p (h i) -> p h i", i=GLA_C),
                                over(masks[rows, P + r:P + r + GLA_C], GLA_H), ALU.mult).then_inc(att_ok, 1)
                ve.drain().then_inc(drained[4], 1)
                if c < NC - 1:
                    for b in (5, 6):
                        bank(b)
                        for h in (2 * (b - 5), 2 * (b - 5) + 1):
                            src = PS[:, b, (h % 2) * GLA_DV:(h % 2 + 1) * GLA_DV]
                            out = state[:, (c + 1) % 2, h, :]
                            if c == 0:
                                ins = v.tensor_copy(out, src)
                            else:
                                ins = v.scalar_tensor_tensor(out=out, in0=state[:, c % 2, h, :],
                                                             scalar=e_end[:, h, c:c + 1], in1=src,
                                                             op0=ALU.mult, op1=ALU.add)
                        ins.then_inc(drained[b], 1)
                    ve.drain().then_inc(st_ok, 1)
                    fence()
                if c % 2 == 0 and c:
                    gla_out(c // 2 - 1)
            gla_out(NT - 1)
            for g in range(2):
                for tc in range(NT):
                    b = 4 * g + tc
                    ve.wait_ge(sil_ok, n.up(sil_ok))
                    out = go[:, tc, half(g)]
                    v.tensor_tensor(out, out, sil[:, tc % 2, :], ALU.mult).then_inc(sil_used, 1)
                    ve.drain().then_inc(drained[b], 1)
                    if g:
                        ve.drain().then_inc(go_ok, 1)
            lo_of_xT()
            layer_norm(ln_p2, ALPHA_2, gate1[:, 0, :])
            modulated(1)
            own(v.memset(u_pad[:, 0:2], 0.0))
            done = 0
            for part, kf in enumerate(KF2):
                with n.loop(ve, kf // 2) as i:
                    for u in range(2):
                        f, dst = bass.ds(i * 2 + (u + done), 1), bass.ds(i * 2 + u, 1)
                        ve.wait_ge(u_ok, n.up(u_ok))
                        taps = [conv[:, f, j] for j in range(4)]
                        own(v.tensor_scalar(u_conv[:, 1, :], u_pad[:, 2:2 + S], taps[2], taps[3], ALU.mult, ALU.add))
                        own(v.scalar_tensor_tensor(out=u_conv[:, 1, :], in0=u_pad[:, 1:1 + S], scalar=taps[1],
                                                   in1=u_conv[:, 1, :], op0=ALU.mult, op1=ALU.add))
                        v.scalar_tensor_tensor(out=u_conv[:, 1, :], in0=u_pad[:, 0:S], scalar=taps[0],
                                               in1=u_conv[:, 1, :], op0=ALU.mult, op1=ALU.add).then_inc(cv_ok, 1)
                        ve.drain().then_inc(drained[4 + 2 * u], 1)
                        ve.wait_ge(su_ok, n.up(su_ok))
                        bank(5 + 2 * u)
                        own(v.tensor_tensor(tmp[:, :], PS[:, 5 + 2 * u, :], u_conv[:, 0, :], ALU.mult))
                        ve.sem_inc(drained[5 + 2 * u], 1)
                        own(v.tensor_copy(hid2_hi[:, dst, :], tmp[:, :].unsqueeze(1)))
                        v.tensor_tensor(hid2_lo[:, dst, :], tmp[:, :].unsqueeze(1),
                                        hid2_hi[:, dst, :].bitcast(F32), ALU.subtract).then_inc(hid_ok, 1)
                        fence()
                done += kf
                if part == 0:
                    for g in range(2):
                        for tc in range(NT):
                            add_to_x(tc, g, ALPHA_2, gate1[:, 1, :])
            layer_norm(ln_p2, 1.0, gate1[:, 1, :])


def tables():
    f32 = np.float32
    p = np.arange(P)
    masks = np.zeros((P, 2 * P), f32)
    masks[:, :P] = np.where(p[None, :] <= p[:, None], 0.0, MASKED)
    masks[:, P:] = (p[:, None] <= p[None, :]) & (p[:, None] // GLA_C == p[None, :] // GLA_C)
    inv_freq = f32(10000.0) ** (-np.arange(RET_D // 2, dtype=f32) / f32(RET_D // 2))
    angle = (np.arange(S, dtype=f32)[:, None] * inv_freq[None, :]).astype(f32).astype(np.float64)
    cos, sin = (f(angle).astype(f32).reshape(NT, P, RET_D // 2).transpose(1, 0, 2) for f in (np.cos, np.sin))
    gamma = 1.0 - 2.0 ** (-5.0 - np.arange(RET_H))
    steps = np.arange(S)[None, :] - p[:, None]
    decay = np.where(steps >= 0, gamma[:, None, None] ** np.maximum(steps, 0), 0.0) * RET_D ** -0.5
    return {
        "ident": np.eye(P, dtype=f32),
        "masks": masks,
        "cos": np.ascontiguousarray(cos),
        "sin": np.ascontiguousarray(np.stack([-sin, sin], 2)),
        "decay": np.ascontiguousarray(decay.transpose(1, 0, 2).astype(f32)),
    }


def across_units(w):
    return w.reshape(KD, P, -1, P).transpose(2, 1, 0, 3).reshape(-1, P, UNIT)


def down_units(w):
    return w.reshape(-1, 2, P, w.shape[1] // HALF, HALF).transpose(3, 0, 2, 1, 4).reshape(-1, P, UNIT)


def narrow_weights(w):
    return np.ascontiguousarray(w.reshape(KD, P, -1).transpose(1, 0, 2).reshape(P, -1))


def lay_out(a):
    fox, ret = FOX_H * FOX_D, RET_H * RET_D
    units, forget = [], []
    for i in range(LAYERS):
        w = a["w_in"][i]
        units.append(across_units(w[:, :2 * fox]))
        units.append(down_units(w[:, 2 * fox:3 * fox]))
        forget.append(narrow_weights(w[:, 3 * fox:3 * fox + FOX_H]))
        units.append(down_units(w[:, 3 * fox + FOX_H:]))
        units.append(down_units(a["w_out"][i]))
        part = KF * P
        for j in range(2):
            units.append(across_units(a["w_ff1"][i][:, j * part:(j + 1) * part]))
            units.append(down_units(a["w_ff2"][i][j * part:(j + 1) * part]))
    w = a["gla_w_in_2"][0]
    qk, dv = GLA_H * GLA_DK, GLA_H * GLA_DV
    units.append(across_units(w[:, :2 * qk]))
    units.append(down_units(w[:, 2 * qk:2 * qk + 2 * dv]))
    units.append(down_units(a["gla_w_o_2"][0]))
    up = across_units(a["ffn_w_up_2"][0]).reshape(2, FF2 // P, P, UNIT).transpose(1, 0, 2, 3)
    at = 0
    for kf in KF2:
        units.append(up[at:at + kf].reshape(-1, P, UNIT))
        units.append(down_units(a["ffn_w_down_2"][0][at * P:(at + kf) * P]))
        at += kf
    mod_b = a["mod_b_2"][0]
    taps = np.concatenate([a["ffn_conv_w_2"][0], a["ffn_conv_b_2"]], 0)
    laid = {
        "x": a["x"][0],
        "stream": np.concatenate(units, 0),
        "w_forget": np.stack(forget),
        "b_forget": a["b_forget"][:, :, None],
        "gn_g": a["ret_gn_g"].reshape(LAYERS, 1, ret),
        "c": a["c_2"][0].reshape(KD, P).T,
        "mod": a["mod_w_2"][0].reshape(2, KD, P, MOD_GROUPS, HALF).transpose(0, 3, 1, 2, 4),
        "mod_bias": mod_b[:, :2 * D].reshape(2, 16, P).transpose(2, 0, 1),
        "gate_bias": mod_b[:, 2 * D:],
        "conv": taps.reshape(4, FF2 // P, P).transpose(2, 1, 0),
        "w_a": narrow_weights(w[:, 2 * qk + 2 * dv:]),
        "w_a2": a["gla_w_a2_2"][0],
        "b_a": a["gla_b_a_2"],
        "norm_g": a["gla_norm_g_2"],
        "ln_g_2": a["ln_g_2"][0],
        "ln_b_2": a["ln_b_2"][0],
    }
    for name in ("ln1_g", "ln1_b", "ln2_g", "ln2_b"):
        laid[name] = a[name][:, None, :]
    return {k: np.ascontiguousarray(v) for k, v in laid.items()}


def add_program(nc, shapes, per_turn):
    t = {k: nc.dram_tensor(f"in_{k}", s, F32, kind="ExternalInput").ap() for k, s in shapes.items()}
    out = nc.dram_tensor("out", (S, D), F32, kind="ExternalOutput").ap()
    t["out"] = out.rearrange("(t p) d -> t p d", p=P)
    t["x"] = t["x"].rearrange("(t p) d -> p t d", p=P)
    t["gate_bias"] = t["gate_bias"].unsqueeze(0).broadcast_to([P, 2, D])
    t["c_scratch"] = nc.dram_tensor("c_scratch", (FOX_H, S), F32, kind="Internal").ap()
    program(nc, t, per_turn)


def kernel(**inputs):
    import concourse.bacc as bacc
    from concourse.bass_utils import run_bass_kernel_spmd

    arrays = {**lay_out({k: np.asarray(v) for k, v in inputs.items()}), **tables()}
    shapes = {k: v.shape for k, v in arrays.items()}
    per_turn = {}
    for _ in range(2):
        nc = bacc.Bacc("TRN2", target_bir_lowering=False, num_devices=1)
        add_program(nc, shapes, per_turn)
    r = run_bass_kernel_spmd(nc, [{f"in_{k}": v for k, v in arrays.items()}], core_ids=[0])
    return r.results[0]["out"].reshape(1, S, D)
```

```python
from contextlib import ExitStack, contextmanager

import numpy as np

import concourse.bass as bass
from concourse import mybir

F32 = mybir.dt.float32
F32R = mybir.dt.float32r
BF16 = mybir.dt.bfloat16
I32 = mybir.dt.int32
ALU = mybir.AluOpType
ACT = mybir.ActivationFunctionType

P = 128
S = 512
NT = S // P
D = 1024
KD = D // P
HALF = 512
LAYERS = 2
FOX_H, FOX_D = 8, 64
RET_H, RET_D = 4, 128
FF = 4 * D
KF = FF // P // 2
GLA_H, GLA_DK, GLA_DV, GLA_C, GLA_RANK = 4, 128, 256, 64, 16
GLA_TAU = 16.0
NC = S // GLA_C
FF2 = 2816
KF2 = (12, 10)
UNIT = 1024
RING = 4
MOD_SLOTS = 4
EPS = 1e-5
ALPHA_1 = float((2 * LAYERS) ** 0.25)
ALPHA_2 = float(2 ** 0.25)
FOX_SCALE = FOX_D ** -0.5
MASKED = -1e30
ROW_OFF = [0, 128, 384, 768]
COL_OFF = [0, 512, 896, 1152]
PACKED = 1280
MOD_GROUPS = 6


class Steps:

    def __init__(self, engine, per_turn):
        self.engine, self.per_turn = engine, per_turn
        self.count, self.loops, self.loops_made = {}, [], 0

    def skip(self, sem, by=1):
        self.count[sem.name] = self.count.get(sem.name, 0) + by

    def at(self, sem, more=0):
        value = self.count.get(sem.name, 0) + more
        for number, i in self.loops:
            turn = self.per_turn.get((self.engine, number, sem.name), 0)
            if turn:
                value = i * turn + value
        return value

    def up(self, sem, by=1):
        self.skip(sem, by)
        return self.at(sem)

    @contextmanager
    def loop(self, eng, turns):
        number, before = self.loops_made, dict(self.count)
        self.loops_made += 1
        with eng.Fori(0, turns) as i:
            self.loops.append((number, i))
            yield i
            self.loops.pop()
        for name, n in list(self.count.items()):
            turn = n - before.get(name, 0)
            self.per_turn[(self.engine, number, name)] = turn
            self.count[name] = before.get(name, 0) + turns * turn


def program(nc, t, per_turn):
    n_units = t["stream"].shape[0]
    ctx = ExitStack()
    with ctx:
        def sb(name, shape, dt=F32):
            return ctx.enter_context(nc.sbuf_tensor(name, shape, dt))

        def sem(name):
            return ctx.enter_context(nc.semaphore(name))

        raw = sb("raw", [P, RING, UNIT])
        w_hi = sb("w_hi", [P, RING, UNIT], F32R)
        w_lo = sb("w_lo", [P, RING, UNIT], F32R)
        x = sb("x", [P, NT, D])
        xT_hi = sb("xT_hi", [P, KD, S], F32R)
        xT_lo = sb("xT_lo", [P, KD, S], F32R)
        ident = sb("ident", [P, P])
        same_chunk = sb("same_chunk", [P, P])
        ident_b = sb("ident_b", [P, P], BF16)
        mask_b = sb("mask_b", [P, P], BF16)
        cos_t = sb("cos_t", [P, NT, RET_D // 2])
        sin_t = sb("sin_t", [P, NT, 2, RET_D // 2])
        ones = sb("ones", [P, P])
        zero = sb("zero", [P, 1])
        wf_raw = sb("wf_raw", [P, KD * FOX_H])
        wf_hi = sb("wf_hi", [P, (KD - 1) * FOX_H + P], F32R)
        wf_lo = sb("wf_lo", [P, (KD - 1) * FOX_H + P], F32R)
        wa_raw = sb("wa_raw", [P, KD * GLA_RANK])
        wa_hi = sb("wa_hi", [P, (KD - 1) * GLA_RANK + P], F32R)
        wa_lo = sb("wa_lo", [P, (KD - 1) * GLA_RANK + P], F32R)
        b_forget = sb("b_forget", [FOX_H, 1])
        gate1 = sb("gate1", [P, 2, D])
        mod_col = sb("mod_col", [P, 3, 16])
        ln_col = sb("ln_col", [P, 2, 2, KD])
        use_col = sb("use_col", [P, 2, KD])
        m = sb("m", [P, 4, 2 * P])
        mod_bias = sb("mod_bias", [P, 2, 16])
        c_col = sb("c_col", [P, KD])
        conv = sb("conv", [P, sum(KF2), 4])
        tmp = sb("tmp", [P, 512])
        small = sb("small", [P, 148])
        row_max, neg_max, row_sum, row_inv = (small[:, 4 * i:4 * i + 4] for i in range(4))
        ln_sum = small[:, 16:24].rearrange("p (t h) -> p t h", h=2)
        ln_nmean, ln_ssq, nmr = small[:, 24:28], small[:, 28:32], small[:, 32:36]
        gn_mv = small[:, 36:68].rearrange("p (t h c) -> p t h c", h=RET_H, c=2)
        gn_stats = small[:, 68:92].rearrange("p (t c) -> p t c", c=6)
        var, newton, rstd = small[:, 92:108], small[:, 108:124], small[:, 124:140]
        gn_nmr = newton
        gla_ssq = small[:, 140:148].rearrange("p (a h) -> p a h", h=GLA_H)

        PS = ctx.enter_context(nc.psum_tensor("PS", [P, 8, HALF], F32))

        def stage(*tensors):
            with ExitStack() as own:
                return [own.enter_context(nc.sbuf_tensor(n, s, d)) for n, s, d in tensors]

        mix_hi, P_f, qT, kT, v_fox, PT, mix_lo, rq, rk, rv, gn_g, decay = stage(
            ("mix_hi", [P, 4, S], F32R), ("P_f", [P, PACKED], F32), ("qT", [P, 4, S], F32), ("kT", [P, 4, S], F32),
            ("v_fox", [P, NT, 512], F32), ("PT", [P, 4, S], F32), ("mix_lo", [P, 4, S], F32R),
            ("rq", [P, NT, 512], F32), ("rk", [P, NT, 512], F32), ("rv", [P, NT, 512], F32),
            ("gn_g", [P, RET_H * RET_D], F32),
            ("decay", [P, RET_H, S], F32))
        cneg = m[:, :, :].rearrange("p (a b) s -> p a (b s)", a=2)
        rg = v_fox
        inner = (PT[:, :, :].rearrange("p a b -> p (a b)"), P_f)
        ln_p, hid_hi, hid_lo, mod_raw, mod_acc, relu_t = stage(
            ("ln_p", [P, 2, D], F32), ("hid_hi", [P, KF, S], F32R), ("hid_lo", [P, KF, S], F32R),
            ("mod_raw", [P, MOD_SLOTS, 512], F32), ("mod_acc", [P, 512], F32), ("relu_t", [P, 2, S], F32))
        (state, gq, gk, la, gv, go, bT, e_pos, e_neg, att, e_end, sil, alrT, w_a2, norm_g) = stage(
            ("state", [P, 2, GLA_H, GLA_DV], F32),
            ("gq", [P, GLA_H, S], F32), ("gk", [P, GLA_H, S], F32), ("la", [P, NT, 512], F32),
            ("gv", [P, NT, D], F32), ("go", [P, NT, D], F32),
            ("bT", [P, S], F32), ("e_pos", [P, S], F32), ("e_neg", [P, S], F32),
            ("att", [P, GLA_H, GLA_C], F32), ("e_end", [P, GLA_H, NC], F32),
            ("sil", [P, 2, 512], F32), ("alrT", [GLA_RANK + 1, S], F32),
            ("w_a2", [GLA_RANK + 1, 512], F32), ("norm_g", [P, GLA_DV], F32))
        _, gT_hi, gT_lo = stage(("gT_at", [P, 2, D], F32), ("gT_hi", [P, 4, S], F32R), ("gT_lo", [P, 4, S], F32R))
        kdT = go[:, 0:2, :].rearrange("p a (b s) -> p (a b) s", s=S)
        ln_p2, hid2_hi, hid2_lo, u_pad, u_conv = stage(
            ("ln_p2", [P, 2, D], F32), ("hid2_hi", [P, KF2[0], S], F32R), ("hid2_lo", [P, KF2[0], S], F32R),
            ("u_pad", [P, 2 + S], F32), ("u_conv", [P, 2, S], F32))

        raw_in = [sem(f"raw_in{i}") for i in range(RING)]
        w_hi_done = sem("w_hi_done")
        w_ready = sem("w_ready")
        w_begun = sem("w_begun")
        full_a = [sem(f"full_a{i}") for i in range(8)]
        full_v = [sem(f"full_v{i}") for i in range(8)]
        drained = [sem(f"drained{i}") for i in range(8)]
        a_did = sem("a_did")
        v_did = sem("v_did")
        v_saw, pe_saw = sem("v_saw"), sem("pe_saw")
        ident_in = sem("ident_in")
        const_in = sem("const_in")
        zero_ok = sem("zero_ok")
        const_ok = sem("const_ok")
        x_in = [sem(f"x_in{i}") for i in range(2)]
        gain_ok = sem("gain_ok")
        x_ready = sem("x_ready")
        last_ready = sem("last_ready")
        rs_ok = sem("rs_ok")
        xn_ok = sem("xn_ok")
        aff_ok = sem("aff_ok")
        col_in = sem("col_in")
        col_ok = sem("col_ok")
        hi_ok = sem("hi_ok")
        lay_in = sem("lay_in")
        wf_ok = sem("wf_ok")
        f_log = sem("f_log")
        c_ok = sem("c_ok")
        c_out = sem("c_out")
        cb_in = [sem(f"cb_in{i}") for i in range(2)]
        max_ok = sem("max_ok")
        exp_ok = sem("exp_ok")
        p_ok = sem("p_ok")
        ret_raw = sem("ret_raw")
        rot_ok = sem("rot_ok")
        inner_ok = sem("inner_ok")
        ret_ok = sem("ret_ok")
        gn_ok = sem("gn_ok")
        gn_done = sem("gn_done")
        o_ok = sem("o_ok")
        ln_in = sem("ln_in")
        y_ok = sem("y_ok")
        sq_ok = sem("sq_ok")
        relu_ok = sem("relu_ok")
        hid_ok = sem("hid_ok")
        mod_in = [sem(f"mod_in{i}") for i in range(MOD_SLOTS)]
        mod_used = sem("mod_used")
        modp_in = sem("modp_in")
        cs_ok = sem("cs_ok")
        wa_ok = sem("wa_ok")
        g_in = sem("g_in")
        one_ok = sem("one_ok")
        la_log = sem("la_log")
        la_ok = sem("la_ok")
        b_ok = sem("b_ok")
        e_ok = sem("e_ok")
        qk_ok = sem("qk_ok")
        att_ok = sem("att_ok")
        st_ok = sem("st_ok")
        gsq_ok = sem("gsq_ok")
        sil_ok = sem("sil_ok")
        sil_used = sem("sil_used")
        go_ok = sem("go_ok")
        mx_ok = sem("mx_ok")
        u_ok = sem("u_ok")
        cv_ok = sem("cv_ok")
        su_ok = sem("su_ok")
        out_done = sem("out_done")

        block = ctx.enter_context(nc.Block())

        def fox_bank(h, job):
            return 4 + (7 * h + job) % 3

        BESIDE = (("q", 0, 2), ("q", 2, 2), ("k", 0, 1), ("k", 1, 1), ("k", 2, 1), ("k", 3, 1), ("v", 0, 2),
                  ("v", 2, 2))
        GLA_BANK = (4, 7)
        RET_BANKS = ((4, (0,)), (5, (1, 3)), (6, (2,)))

        def four(bank):
            return PS[:, bank, :].rearrange("p (j c) -> p j c", c=P)

        def chunk(tc):
            return slice(tc * P, (tc + 1) * P)

        def half(g):
            return slice(g * HALF, (g + 1) * HALF)

        def over(ap, count):
            return ap.unsqueeze(1).broadcast_to([ap.shape[0], count, ap.shape[1]])

        @block.sync
        def _(sp):
            n = Steps("sp", per_turn)
            for u in range(RING):
                if u == 2:
                    sp.wait_ge(x_in[0], 32)
                sp.dma_start(raw[:, u, :], t["stream"][u]).then_inc(raw_in[u], 16)
            turns, rest = divmod(n_units - RING, RING)

            def refill(at, u):
                sp.wait_ge(w_ready, n.up(w_ready))
                sp.dma_start(raw[:, u, :], t["stream"][at]).then_inc(raw_in[u], 16)

            with n.loop(sp, turns) as i:
                for u in range(RING):
                    refill(sp.snap(i * RING + (RING + u)), u)
            for u in range(rest):
                refill(RING + turns * RING + u, u)
            for tc in range(NT):
                if tc < NT - 1:
                    sp.wait_ge(x_ready, n.up(x_ready))
                else:
                    sp.wait_ge(last_ready, 1)
                sp.dma_start(t["out"][tc], x[:, tc, :]).then_inc(out_done, 16)
            sp.wait_ge(out_done, 16 * NT)

        @block.gpsimd
        def _(pool):
            n = Steps("pool", per_turn)
            pool.wait_ge(zero_ok, 1)
            n.skip(w_begun, 1)

            def cut(u, again=True):
                pool.wait_ge(raw_in[u], n.up(raw_in[u], 16))
                if again:
                    pool.wait_ge(w_begun, n.up(w_begun))
                nc.gpsimd.tensor_tensor(w_hi[:, u, :], raw[:, u, :], zero[:, 0:1].broadcast_to([P, UNIT]),
                                        ALU.add).then_inc(w_hi_done, 1)
                pool.wait_ge(w_hi_done, n.up(w_hi_done))
                nc.gpsimd.tensor_tensor(w_lo[:, u, :], raw[:, u, :], w_hi[:, u, :].bitcast(F32),
                                        ALU.subtract).then_inc(w_ready, 1)

            for u in range(RING):
                cut(u, again=False)
            turns, rest = divmod(n_units - RING, RING)
            with n.loop(pool, turns):
                for u in range(RING):
                    cut(u)
            for u in range(rest):
                cut(u)
            for tc in range(NT - 1):
                pool.wait_ge(gain_ok, n.up(gain_ok))
                nc.gpsimd.tensor_tensor(x[:, tc, :], x[:, tc, :], ln_p2[:, 1, :], ALU.add).then_inc(x_ready, 1)

        @block.tensor
        def _(pe):
            n = Steps("pe", per_turn)
            units = [0]
            mm, turn = nc.tensor.matmul, nc.tensor.transpose

            def take(b):
                pe.wait_ge(drained[b], n.up(drained[b]))

            def after(b):
                pe.wait_ge(drained[b], n.at(drained[b], 1))

            def next_unit(hi_only=False):
                if hi_only:
                    pe.wait_ge(w_hi_done, n.up(w_hi_done))
                else:
                    n.skip(w_hi_done)
                    pe.wait_ge(w_ready, n.up(w_ready))
                units[0] += 1
                return (units[0] - 1) % RING

            def across(bank):
                take(bank)
                s = next_unit()
                out = PS[:, bank, :]
                for k in range(KD):
                    hi, lo = (w[:, s, chunk(k)] for w in (w_hi, w_lo))
                    ins = mm(out, hi, xT_hi[:, k, :], start=k == 0, stop=False)
                    if k == 0:
                        ins.then_inc(w_begun, 1)
                    mm(out, hi, xT_lo[:, k, :], start=False, stop=False)
                    last = mm(out, lo, xT_hi[:, k, :], start=False, stop=k == KD - 1)
                return last

            def of_x(k, tc):
                return xT_hi[:, k, chunk(tc)], xT_lo[:, k, chunk(tc)]

            def of_mixed(k, tc):
                return (mix_hi[:, k, chunk(tc)], mix_lo[:, k, chunk(tc)]) if k < 4 else of_x(k, tc)

            def of_gated(k, tc):
                return (gT_hi[:, k, chunk(tc)], gT_lo[:, k, chunk(tc)]) if k < 4 else of_x(k, tc)

            def of_hidden(k, tc):
                return hid_hi[:, k, chunk(tc)], hid_lo[:, k, chunk(tc)]

            def of_hidden_2(k, tc):
                return hid2_hi[:, k, chunk(tc)], hid2_lo[:, k, chunk(tc)]

            def down_chunk(a, k0, bank, tc, s, begins, first, last):
                out = PS[:, bank, :]
                for kk in range(2):
                    hi, lo = (w[:, s, half(kk)] for w in (w_hi, w_lo))
                    a_hi, a_lo = a(k0 + kk, tc)
                    ins = mm(out, a_hi, hi, start=first and kk == 0, stop=False)
                    if begins and kk == 0:
                        ins.then_inc(w_begun, 1)
                    mm(out, a_hi, lo, start=False, stop=False)
                    ins = mm(out, a_lo, hi, start=False, stop=last and kk == 1)
                return ins

            def across_halves(full):
                slots = {}
                for p in range(2):
                    cols = slice(2 * P * p, 2 * P * (p + 1))
                    for u in range(RING):
                        if p == 0:
                            take(4 + u)
                            slots[u] = next_unit(hi_only=u > 0)
                        out, slot = PS[:, 4 + u, cols], slots[u]
                        for k in range(KD):
                            if u == 0:
                                modulated_half(p, k)
                            ins = mm(out, w_hi[:, slot, chunk(k)], xT_hi[:, k, cols], start=k == 0, stop=False)
                            if k == 0 and p == (u > 0):
                                ins.then_inc(w_begun, 1)
                            last = mm(out, w_hi[:, slot, chunk(k)], xT_lo[:, k, cols], start=False, stop=False)
                            if u == 0:
                                last = mm(out, w_lo[:, slot, chunk(k)], xT_hi[:, k, cols], start=False,
                                          stop=k == KD - 1)
                        if u and p == 0:
                            pe.wait_ge(w_ready, n.up(w_ready))
                        for k in range(KD if u else 0):
                            last = mm(out, w_lo[:, slot, chunk(k)], xT_hi[:, k, cols], start=False,
                                      stop=k == KD - 1)
                        if p == 0:
                            later_half(u)
                        else:
                            last.then_inc(full[4 + u], 1)

            def down(a, bank0, full, count, of=None, at=0, stagger=False, before=lambda u: None,
                     near_end=lambda: None, before_tile=lambda u, tc: None):
                of = of or count
                for u in range(at, at + count - (RING if stagger else 0)):
                    before(u)
                    s = next_unit()
                    for tc in range(NT):
                        before_tile(u, tc)
                        if u == 0:
                            take(bank0 + tc)
                        ins = down_chunk(a, 2 * u, bank0 + tc, tc, s, tc == 0, u == 0, u == of - 1)
                        if u == of - 1:
                            ins.then_inc(full[bank0 + tc], 1)
                if stagger:
                    slots = {}
                    cells = [(tc, u) for tc in range(NT) for u in range(RING)]
                    cells[3], cells[4] = cells[4], cells[3]
                    for number, (tc, step) in enumerate(cells):
                        u = of - RING + step
                        if number == NT * RING - 2:
                            near_end()
                        if tc == 0:
                            before(u)
                            slots[u] = next_unit()
                        if u == 0:
                            take(bank0 + tc)
                        begins = (tc == 0) if step == 0 else (tc == NT - 1)
                        ins = down_chunk(a, 2 * u, bank0 + tc, tc, slots[u], begins, u == 0, u == of - 1)
                        if u == of - 1:
                            ins.then_inc(full[bank0 + tc], 1)

            def blocks_to_bank(b, blocks):
                take(b)
                for j, src in enumerate(blocks):
                    last = turn(PS[:, b, chunk(j)], src, ident[:, :])
                return last

            def transposed_half(p):
                pe.wait_ge(xn_ok, n.up(xn_ok, 2))
                for b in range(4):
                    blocks_to_bank(b, [x[:, 2 * p + j, chunk(2 * b + i)] for i in range(2)
                                       for j in range(2)]).then_inc(full_a[b], 1)

            def later_chunks(u, tc):
                if u == 2:
                    after(4 + tc)

            def modulated_half(p, k):
                pe.wait_ge(mx_ok, n.up(mx_ok))

            def later_half(u):
                if u == 2:
                    transposed_half(1)

            def first_half():
                transposed_half(0)

            def narrow(bank, hi, lo, m):
                take(bank)
                for k in range(KD):
                    c = slice(k * m, k * m + P)
                    mm(PS[:, bank, :], hi[:, c], xT_hi[:, k, :], start=k == 0, stop=False)
                    mm(PS[:, bank, :], hi[:, c], xT_lo[:, k, :], start=False, stop=False)
                    last = mm(PS[:, bank, :], lo[:, c], xT_hi[:, k, :], start=False, stop=k == KD - 1)
                return last

            def fox_scores(h):
                r, c = FOX_D * (h % 2), h // 2
                for i in range(NT):
                    b, w = fox_bank(h, i), P * (i + 1)
                    take(b)
                    mm(PS[:, b, 0:w], qT[r:r + FOX_D, c, chunk(i)], kT[r:r + FOX_D, c, 0:w],
                       start=True, stop=False)
                    mm(PS[:, b, chunk(i)], ident_b[:, :], mask_b[:, :], start=False,
                       stop=True).then_inc(full_v[b], 1)

            def fox_transposes(h):
                for job, rows in enumerate(((0, 1), (2,), (3,))):
                    pe.wait_ge(p_ok, n.up(p_ok, len(rows)))
                    blocks = [P_f[:, ROW_OFF[i] + j * P:ROW_OFF[i] + (j + 1) * P]
                              for i in rows for j in range(i + 1)]
                    b = fox_bank(h, NT + job)
                    blocks_to_bank(b, blocks).then_inc((full_v if job == 1 else full_a)[b], 1)

            def fox_values(h):
                r = FOX_D * (h % 2)
                if h % 2 == 0:
                    take(7)
                for j in range(NT):
                    last = mm(PS[r:r + FOX_D, 7, j * P:S], v_fox[:, j, h * FOX_D:(h + 1) * FOX_D],
                              PT[:, j, j * P:S], start=j == 0, stop=j == NT - 1)
                if h % 2:
                    last.then_inc(full_v[7], 1)

            def ret_scores(h):
                for b, blocks in RET_BANKS:
                    take(b)
                    at = 0
                    for j in blocks:
                        w = S - j * P
                        last = mm(PS[:, b, at:at + w], kT[:, h, chunk(j)], qT[:, h, j * P:S],
                                  start=True, stop=True)
                        at += w
                    last.then_inc(full_v[b], 1)

            def ret_values(h):
                take(7)
                pe.wait_ge(inner_ok, n.up(inner_ok, NT))
                for i in range(NT):
                    for j in range(i + 1):
                        o = COL_OFF[j] + (i - j) * P
                        last = mm(PS[:, 7, chunk(i)], inner[h % 2][:, o:o + P], rv[:, j, chunk(h)],
                                  start=j == 0, stop=j == i)
                last.then_inc(full_a[7], 1)

            def mod_reduce(g):
                pe.wait_ge(mod_used, n.up(mod_used, KD))
                take(4)
                if g < 4:
                    for j in range(4):
                        last = mm(PS[:, 4, j:j + 1], mod_acc[:, chunk(j)], ones[:, 0:1], start=True, stop=True)
                else:
                    last = mm(PS[:, 4, :], ones[:, :], mod_acc[:, :], start=True, stop=True)
                last.then_inc(full_v[4], 1)

            pe.wait_ge(ident_in, 16)
            transposed_half(0)
            n.skip(mod_used, MOD_SLOTS)
            with n.loop(pe, LAYERS):
                across_halves(full_a)
                pe.wait_ge(const_ok, 1)
                pe.wait_ge(wf_ok, n.up(wf_ok))
                narrow(0, wf_hi, wf_lo, FOX_H).then_inc(full_a[0], 1)
                for b in range(4, 8):
                    across(b).then_inc(full_v[b], 1)
                down(of_x, 0, full_a, 4)
                for b in range(4, 8):
                    after(b)
                fox_scores(0)
                for h in range(FOX_H):
                    down(of_x, 0, full_a, BESIDE[h][2], of=4, at=BESIDE[h][1])
                    fox_transposes(h)
                    if h + 1 < FOX_H:
                        fox_scores(h + 1)
                    else:
                        for job in range(3):
                            after(fox_bank(h, NT + job))
                    fox_values(h)
                for src, full in ((rq, full_v), (rk, full_a)):
                    pe.wait_ge(rot_ok, n.up(rot_ok, NT))
                    for h in range(RET_H):
                        b = h + (4 if src is rq else 0)
                        blocks_to_bank(b, [src[:, tc, chunk(h)] for tc in range(NT)]).then_inc(full[b], 1)
                after(0)
                ret_scores(0)
                for h in range(RET_H):
                    down(of_x, 0, full_a, 1, of=4, at=h)
                    if h + 1 < RET_H:
                        ret_scores(h + 1)
                    ret_values(h)
                down(of_mixed, 0, full_v, 2, of=4)
                for tc in range(NT):
                    pe.wait_ge(ret_ok, n.up(ret_ok))
                    b = 4 + tc
                    blocks_to_bank(b, [rq[:, tc, chunk(h)] for h in range(RET_H)]).then_inc(full_a[b], 1)
                down(of_mixed, 0, full_v, 2, of=4, at=2, before_tile=later_chunks)

                down(of_mixed, 4, full_v, 4, stagger=True, near_end=first_half)
                across_halves(full_a)
                for part in range(2):
                    pe.sem_inc(pe_saw, 1)
                    with n.loop(pe, KF // RING - (part == 0)):
                        for u in range(RING):
                            across(u).then_inc(full_a[u], 1)

                    def before_down(u):
                        pe.wait_ge(hid_ok, n.up(hid_ok, 2))
                        if u in (3, 5, 7):
                            mod_reduce(3 * part + u // 2 - 1)

                    down(of_hidden, 0, full_v, KF // 2, before=before_down)
                    down(of_hidden, 4, full_v, KF // 2, stagger=part == 1,
                         near_end=first_half)

            across_halves(full_a)
            pe.wait_ge(wa_ok, 1)
            narrow(0, wa_hi, wa_lo, GLA_RANK).then_inc(full_v[0], 1)
            for b in range(4, 8):
                across(b).then_inc(full_v[b], 1)
            after(0)
            pe.wait_ge(g_in, 16 * 3)
            for tc in range(NT):
                take(tc)
                mm(PS[:, tc, :], alrT[:, chunk(tc)], w_a2[:, :], start=True, stop=True).then_inc(full_a[tc], 1)
            down(of_x, 4, full_a, 4)
            pe.wait_ge(la_ok, n.up(la_ok, NT))

            def gate_sums(h):
                b = 4 + h % 2
                take(b)
                for tc in range(NT):
                    last = mm(PS[:, b, chunk(tc)], la[:, tc, chunk(h)], same_chunk[:, :], start=True, stop=True)
                last.then_inc(full_v[b], 1)

            down(of_x, 0, full_a, 4, before=gate_sums)
            for h in range(GLA_H):
                pe.wait_ge(qk_ok, n.up(qk_ok))
                b = 6 + h % 2
                blocks_to_bank(b, [kdT[:, h, chunk(tc)] for tc in range(NT)]).then_inc(full_a[b], 1)
            for b in (0, 1, 2, 3, 6, 7):
                after(b)

            def gla_scores(c):
                b, r = GLA_BANK[c % 2], GLA_C * (c % 2)
                tok = slice(c * GLA_C, (c + 1) * GLA_C)
                take(b)
                for h in range(GLA_H):
                    last = mm(PS[r:r + GLA_C, b, h * GLA_C:(h + 1) * GLA_C], gk[:, h, tok], gq[:, h, tok],
                              start=True, stop=True)
                last.then_inc(full_v[b], 1)

            gla_scores(0)
            for c in range(NC):
                tc, r = c // 2, GLA_C * (c % 2)
                rows, tok = slice(r, r + GLA_C), slice(c * GLA_C, (c + 1) * GLA_C)
                if c + 1 < NC:
                    gla_scores(c + 1)
                if c < NC - 1:
                    for h in range(GLA_H):
                        b = 5 + h // 2
                        if h % 2 == 0:
                            take(b)
                        last = mm(PS[:, b, (h % 2) * GLA_DV:(h % 2 + 1) * GLA_DV], la[rows, tc, chunk(h)],
                                  gv[rows, tc, h * GLA_DV:(h + 1) * GLA_DV], start=True, stop=True)
                        if h % 2:
                            last.then_inc(full_v[b], 1)
                o_bank = 2 * (tc % 2)
                if c % 2 == 0:
                    take(o_bank)
                    take(o_bank + 1)
                pe.wait_ge(att_ok, n.up(att_ok))
                if c:
                    pe.wait_ge(st_ok, n.up(st_ok))
                for h in range(GLA_H):
                    out = PS[rows, o_bank + h // 2, (h % 2) * GLA_DV:(h % 2 + 1) * GLA_DV]
                    last = mm(out, att[rows, h, :], gv[rows, tc, h * GLA_DV:(h + 1) * GLA_DV],
                              start=True, stop=c == 0)
                    if c:
                        last = mm(out, gq[:, h, tok], state[:, c % 2, h, :], start=False, stop=True)
                    if c % 2 and h % 2:
                        last.then_inc(full_a[o_bank + h // 2], 1)
            def go_transposed(g):
                for tc in range(NT):
                    pe.wait_ge(go_ok, n.up(go_ok))
                    blocks_to_bank(4 + tc, [go[:, tc, chunk(4 * g + j)] for j in range(4)]).then_inc(full_a[4 + tc], 1)

            down(of_x, 4, full_a, 4)
            down(of_x, 0, full_a, 4, before=lambda u: go_transposed(0) if u == 2 else None)
            for b in range(4, 8):
                after(b)
            down(of_gated, 0, full_v, 1, of=4)
            go_transposed(1)
            down(of_gated, 0, full_v, 1, of=4, at=1)
            down(of_gated, 0, full_v, 2, of=4, at=2, before_tile=later_chunks)
            down(of_gated, 4, full_v, 4, stagger=True, near_end=first_half)
            across_halves({b: (full_v if b % 2 else full_a)[b] for b in range(4, 8)})
            for part, kf in enumerate(KF2):
                with n.loop(pe, kf // 2 - (part == 0)):
                    for u in range(RING):
                        b = 4 + u
                        across(b).then_inc((full_v if u % 2 else full_a)[b], 1)
                down(of_hidden_2, 0, full_v, kf // 2,
                     before=lambda u: pe.wait_ge(hid_ok, n.up(hid_ok, 2)))
                down(of_hidden_2, 4, full_v, kf // 2, stagger=part == 1)

        @block.scalar
        def _(act):
            n = Steps("act", per_turn)
            run = nc.scalar.activation

            def own(ins):
                ins.then_inc(a_did, 1)
                act.wait_ge(a_did, n.up(a_did))

            def bank(b):
                act.wait_ge(full_a[b], n.up(full_a[b]))

            def modulated(p, gain, bias):
                for k in range(KD):
                    b, cols = k // 2, slice(2 * P * p, 2 * P * (p + 1))
                    src = PS[:, b, 2 * P * (k % 2):2 * P * (k % 2 + 1)]
                    if k % 2 == 0:
                        bank(b)
                    factors = dict(scale=gain[:, k:k + 1], bias=bias[:, k:k + 1])
                    if k % 2 == 0:
                        if p or k >= 4:
                            act.wait_ge(mx_ok, n.at(mx_ok, 1))
                        run(m[:, k % 4, :], src, ACT.Identity, **factors)
                    if p or k >= 4:
                        n.skip(mx_ok)
                    run(xT_hi[:, k, cols], src, ACT.Identity, **factors).then_inc(hi_ok, 1)
                if p:
                    n.skip(mx_ok, 4)

            def squares(junk, tc):
                act.wait_ge(y_ok, n.up(y_ok))
                run(junk, x[:, tc, :], ACT.Square, bias=ln_nmean[:, tc:tc + 1],
                    accum_out=ln_ssq[:, tc:tc + 1]).then_inc(sq_ok, 1)
                act.wait_ge(sq_ok, n.up(sq_ok))

            def normalised(tc):
                act.wait_ge(rs_ok, n.up(rs_ok))
                run(x[:, tc, :], x[:, tc, :], ACT.Identity, scale=rstd[:, tc:tc + 1],
                    bias=nmr[:, tc:tc + 1]).then_inc(xn_ok, 1)

            def layer_norm(junk, gain, bias):
                for tc in range(3):
                    squares(junk, tc)
                    if tc == 2:
                        modulated(0, gain, bias)
                    normalised(tc)
                squares(junk, 3)
                normalised(3)

            def load_ln(g, b, dst):
                act.dma_start(dst[:, 0, :], g.broadcast_to([P, D])).then_inc(ln_in, 16)
                act.dma_start(dst[:, 1, :], b.broadcast_to([P, D])).then_inc(ln_in, 16)

            act.dma_start(ident[:], t["ident"]).then_inc(ident_in, 16)
            act.dma_start(use_col[:, :, :], t["ln_cols"][0]).then_inc(col_in, 16)
            for tc in range(NT):
                act.dma_start(x[:, tc, :], t["x"][:, tc, :]).then_inc(x_in[tc // 2], 16)
            for name, dst in (("same_chunk", same_chunk), ("causal", tmp[:, 0:P]), ("cos", cos_t), ("sin", sin_t)):
                act.dma_start(dst[:], t[name]).then_inc(const_in, 16)
            for name, dst in (("c", c_col), ("mod_bias", mod_bias), ("gate_bias", gate1), ("conv", conv),
                              ("w_a", wa_raw)):
                act.dma_start(dst[:], t[name]).then_inc(modp_in, 16)
            act.wait_ge(col_in, n.up(col_in, 16))
            modulated(0, use_col[:, 0, :], use_col[:, 1, :])
            act.wait_ge(modp_in, 16 * 5)
            run(c_col[:, :], c_col[:, :], ACT.Silu).then_inc(cs_ok, 1)
            with n.loop(act, LAYERS) as layer:
                act.dma_start(ln_col[:, 0], t["ln_cols"][layer * 2 + 1]).then_inc(col_in, 16)
                act.dma_start(ln_col[:, 1], t["ln_cols"][layer * 2 + 2]).then_inc(col_in, 16)
                act.dma_start(wf_raw[:, :], t["w_forget"][layer]).then_inc(lay_in, 16)
                act.dma_start(b_forget[:, :], t["b_forget"][layer]).then_inc(lay_in, 16)
                act.dma_start(gn_g[:, :], t["gn_g"][layer].broadcast_to([P, RET_H * RET_D])).then_inc(lay_in, 16)
                act.dma_start(decay[:, :, :], t["decay"]).then_inc(lay_in, 16)
                modulated(1, use_col[:, 0, :], use_col[:, 1, :])
                for u in range(4):
                    b = 4 + u
                    bank(b)
                    run(qT[:, u, :], PS[:, b, :], ACT.Copy).then_inc(drained[b], 1)
                act.wait_ge(lay_in, n.up(lay_in, 16 * 4))
                bank(0)
                fe = P_f[0:FOX_H, 0:S]
                own(run(fe, PS[0:FOX_H, 0, :], ACT.Abs, bias=b_forget[:, 0:1]))
                own(run(fe, fe, ACT.Exp, scale=-1.0))
                run(fe, fe, ACT.Ln, bias=1.0).then_inc(f_log, 1)
                act.wait_ge(c_ok, n.up(c_ok))
                act.dma_start(t["c_scratch"], P_f[0:FOX_H, S:2 * S]).then_inc(c_out, 16)
                act.wait_ge(c_out, n.up(c_out, 16))

                def load_c(h):
                    act.dma_start(cneg[:, h % 2, :], t["c_scratch"][h:h + 1, :].broadcast_to([P, S])).then_inc(
                        cb_in[h % 2], 16)

                def projection_out(dst, function):
                    for b in range(4):
                        bank(b)
                        run(dst[:, b, :], PS[:, b, :], function).then_inc(drained[b], 1)
                    act.drain().then_inc(ret_raw, 1)

                load_c(0)
                load_c(1)
                for b in range(4):
                    bank(b)
                    run(v_fox[:, b, :], PS[:, b, :], ACT.Copy).then_inc(drained[b], 1)
                for h in range(FOX_H):
                    act.wait_ge(max_ok, n.up(max_ok))
                    if h + 2 < FOX_H:
                        load_c(h + 2)
                    for i in range(NT):
                        rows = P_f[:, ROW_OFF[i]:ROW_OFF[i] + P * (i + 1)]
                        run(rows, rows, ACT.Exp, bias=neg_max[:, i:i + 1], scale=FOX_SCALE,
                            accum_out=row_sum[:, i:i + 1]).then_inc(exp_ok, 1)
                    b = fox_bank(h, NT)
                    bank(b)
                    run(PT[:, 0, 0:P], PS[:, b, 0:P], ACT.Copy)
                    run(PT[:, 0:2, P:2 * P], four(b)[:, 1:3, :], ACT.Copy).then_inc(drained[b], 1)
                    b = fox_bank(h, NT + 2)
                    bank(b)
                    run(PT[:, :, 3 * P:], four(b), ACT.Copy).then_inc(drained[b], 1)
                    which, at, count = BESIDE[h]
                    if at + count == 4:
                        projection_out({"q": rq, "k": rk, "v": rv}[which], ACT.Copy)
                for h in range(RET_H):
                    bank(h)
                    run(kT[:, h, :], PS[:, h, :], ACT.Copy).then_inc(drained[h], 1)
                for h in range(RET_H):
                    if h == RET_H - 1:
                        projection_out(rg, ACT.Silu)
                    bank(7)
                    run(rq[:, :, chunk(h)], four(7), ACT.Copy).then_inc(drained[7], 1)
                    act.drain().then_inc(o_ok, 1)
                act.wait_ge(gn_ok, n.up(gn_ok))
                for tc in (1, 3):
                    for h in range(RET_H):
                        col = slice(RET_H * tc + h, RET_H * tc + h + 1)
                        run(rq[:, tc, chunk(h)], rq[:, tc, chunk(h)], ACT.Identity, scale=rstd[:, col],
                            bias=gn_nmr[:, col])
                    act.drain().then_inc(gn_done, 1)
                for tc in range(NT):
                    b = 4 + tc
                    bank(b)
                    run(xT_hi[:, 4:8, chunk(tc)], four(b), ACT.Copy).then_inc(hi_ok, 1)
                junk = relu_t[:, :, :].rearrange("p a b -> p (a b)")
                act.wait_ge(col_in, n.up(col_in, 32))
                gain, bias = ln_col[:, 0, 0], ln_col[:, 0, 1]
                layer_norm(junk, gain, bias)
                act.wait_ge(aff_ok, n.up(aff_ok))
                load_ln(t["ln1_g"][layer], t["ln1_b"][layer], ln_p)
                modulated(1, gain, bias)

                def load_mod(number):
                    g, k = divmod(number, KD)
                    slot = number % MOD_SLOTS
                    act.wait_ge(mod_used, n.up(mod_used))
                    act.dma_start(mod_raw[:, slot, :], t["mod"][layer, g, k]).then_inc(mod_in[slot], 16)

                for number in range(MOD_SLOTS):
                    load_mod(number)

                def relu(b, u, again=True):
                    bank(b)
                    if again:
                        act.wait_ge(hid_ok, n.up(hid_ok))
                    run(relu_t[:, u % 2, :], PS[:, b, :], ACT.Relu).then_inc(relu_ok, 1)

                for u in range(RING):
                    relu(4 + u, u, again=u >= 2)
                for part in range(2):
                    with n.loop(act, KF // RING - (part == 0)):
                        for u in range(RING):
                            relu(u, u)
                    for number in range(3 * KD):
                        number += 3 * KD * part + MOD_SLOTS
                        if number < MOD_GROUPS * KD:
                            load_mod(number)
                    if part == 0:
                        act.wait_ge(aff_ok, n.up(aff_ok))
                        load_ln(t["ln2_g"][layer], t["ln2_b"][layer], ln_p)
                n.skip(hid_ok, 2)
                act.wait_ge(col_ok, n.up(col_ok))
                layer_norm(junk, use_col[:, 0, :], use_col[:, 1, :])

            act.dma_start(w_a2[0:GLA_RANK, :], t["w_a2"]).then_inc(g_in, 16)
            act.dma_start(w_a2[GLA_RANK:GLA_RANK + 1, :], t["b_a"]).then_inc(g_in, 16)
            act.dma_start(norm_g[:, :], t["norm_g"].broadcast_to([P, GLA_DV])).then_inc(g_in, 16)
            modulated(1, use_col[:, 0, :], use_col[:, 1, :])
            act.dma_start(ln_col[:, 0], t["ln_cols"][2 * LAYERS + 1]).then_inc(col_in, 16)
            for u in range(4):
                b = 4 + u
                bank(b)
                run(gq[:, u, :], PS[:, b, :], ACT.Copy, scale=GLA_DK ** -0.5).then_inc(drained[b], 1)
            for tc in range(NT):
                bank(tc)
                own(run(la[:, tc, :], PS[:, tc, :], ACT.Abs))
            own(run(la[:, :, :], la[:, :, :], ACT.Exp, scale=-1.0))
            run(la[:, :, :], la[:, :, :], ACT.Ln, bias=1.0).then_inc(la_log, 1)
            for tc in range(NT):
                bank(4 + tc)
                run(gv[:, tc, half(0)], PS[:, 4 + tc, :], ACT.Copy).then_inc(drained[4 + tc], 1)
            for h in range(GLA_H):
                act.wait_ge(b_ok, n.up(b_ok))
                run(e_pos[:, :], bT[:, :], ACT.Exp, scale=1 / GLA_TAU)
                run(e_neg[:, :], bT[:, :], ACT.Exp, scale=-1 / GLA_TAU)
                run(e_end[:, h, :], bT[:, :].rearrange("p (c s) -> p c s", s=GLA_C)[:, :, GLA_C - 1],
                    ACT.Exp, scale=1 / GLA_TAU)
                run(kdT[:, h, :], kdT[:, h, :], ACT.Exp, scale=1 / GLA_TAU).then_inc(e_ok, 1)
            for tc in range(NT):
                bank(tc)
                run(gv[:, tc, half(1)], PS[:, tc, :], ACT.Copy).then_inc(drained[tc], 1)
            for h in range(GLA_H):
                b = 6 + h % 2
                bank(b)
                run(la[:, :, chunk(h)], four(b), ACT.Copy).then_inc(drained[b], 1)
            for tc in range(NT):
                for h in range(GLA_H):
                    b = 2 * (tc % 2) + h // 2
                    if h % 2 == 0:
                        bank(b)
                    ins = run(m[:, h, :], PS[:, b, (h % 2) * GLA_DV:(h % 2 + 1) * GLA_DV],
                              ACT.Square, accum_out=gla_ssq[:, tc % 2, h:h + 1])
                ins.then_inc(gsq_ok, 1)
                act.wait_ge(gsq_ok, n.up(gsq_ok))
            for g in range(2):
                for tc in range(NT):
                    b = 4 * (1 - g) + tc
                    bank(b)
                    act.wait_ge(sil_used, n.up(sil_used))
                    run(sil[:, tc % 2, :], PS[:, b, :], ACT.Silu).then_inc(sil_ok, 1)
                for tc in range(NT):
                    bank(4 + tc)
                    dst = xT_hi[:, 4:8, chunk(tc)] if g else gT_hi[:, :, chunk(tc)]
                    run(dst, four(4 + tc), ACT.Copy).then_inc(hi_ok, 1)
            load_ln(t["ln_g_2"][0:1, :], t["ln_b_2"][0:1, :], ln_p2)
            act.wait_ge(col_ok, n.up(col_ok))
            junk = u_conv[:, :, :].rearrange("p a b -> p (a b)")
            layer_norm(junk, use_col[:, 0, :], use_col[:, 1, :])
            modulated(1, use_col[:, 0, :], use_col[:, 1, :])

            def branch(u):
                bank(4 + 2 * u)
                run(u_pad[:, 2:2 + S], PS[:, 4 + 2 * u, :], ACT.Copy).then_inc(u_ok, 1)
                act.wait_ge(cv_ok, n.up(cv_ok))
                run(u_conv[:, 0, :], u_conv[:, 1, :], ACT.Silu).then_inc(su_ok, 1)

            for u in range(2):
                branch(u)
            for part, kf in enumerate(KF2):
                if part:
                    act.wait_ge(aff_ok, n.up(aff_ok, 2))
                    load_ln(t["ln_g_2"][1:2, :], t["ln_b_2"][1:2, :], ln_p2)
                with n.loop(act, kf // 2 - (part == 0)):
                    for u in range(2):
                        branch(u)
            for tc in range(NT):
                squares(junk, tc)
                normalised(tc)

        @block.vector
        def _(ve):
            n = Steps("ve", per_turn)
            v = nc.vector

            def own(ins):
                ins.then_inc(v_did, 1)
                ve.wait_ge(v_did, n.up(v_did))

            def fence():
                ve.drain().then_inc(v_did, 1)
                ve.wait_ge(v_did, n.up(v_did))

            def bank(b):
                ve.wait_ge(full_v[b], n.up(full_v[b]))

            def settled():
                ve.sem_inc(v_saw, 1)

            def modulated(p, gain, bias):
                for k in range(KD):
                    b, cols = k // 2, slice(2 * P * p, 2 * P * (p + 1))
                    ve.wait_ge(hi_ok, n.up(hi_ok))
                    if k % 2:
                        own(v.tensor_scalar(m[:, k % 4, :], PS[:, b, 2 * P:4 * P], gain[:, k:k + 1],
                                            bias[:, k:k + 1], ALU.mult, ALU.add))
                        ve.sem_inc(drained[b], 1)
                    v.tensor_tensor(xT_lo[:, k, cols], m[:, k % 4, :], xT_hi[:, k, cols].bitcast(F32),
                                    ALU.subtract).then_inc(mx_ok, 1)

            def rsqrt_col(out, arg, by):
                v.tensor_scalar(by[:, 1:2], arg, -0.5, None, ALU.mult)
                by, less = by[:, 0:1], by[:, 1:2]
                own(v.tensor_scalar(by.bitcast(I32), arg.bitcast(I32), 1, None, ALU.logical_shift_right))
                own(v.tensor_scalar(out.bitcast(I32), by.bitcast(I32), -1.0, 1597463007.0, ALU.mult, ALU.add))
                for _ in range(3):
                    own(v.scalar_tensor_tensor(out=by, in0=out, scalar=less, in1=out, op0=ALU.mult, op1=ALU.mult))
                    own(v.scalar_tensor_tensor(out=out, in0=by, scalar=1.5, in1=out, op0=ALU.add, op1=ALU.mult))

            def rsqrt(out, arg, by):
                own(v.tensor_scalar(by.bitcast(I32), arg.bitcast(I32), 1, None, ALU.logical_shift_right))
                own(v.tensor_scalar(out.bitcast(I32), by.bitcast(I32), -1.0, 1597463007.0, ALU.mult, ALU.add))
                for _ in range(3):
                    own(v.tensor_tensor(by, out, out, ALU.mult))
                    own(v.tensor_tensor(by, by, arg, ALU.mult))
                    own(v.tensor_scalar(by, by, -0.5, 1.5, ALU.mult, ALU.add))
                    own(v.tensor_tensor(out, out, by, ALU.mult))

            def add_to_x(tc, g, scale, gate=None, b=None, accumulate=False):
                b = 4 * g + tc if b is None else b
                bank(b)
                src = PS[:, b, :]
                if gate is not None:
                    own(v.tensor_tensor(tmp[:, :], src, gate[:, half(g)], ALU.mult))
                    src = tmp[:, :]
                out = x[:, tc, half(g)]
                v.scalar_tensor_tensor(out=out, in0=out, scalar=scale, in1=src, op0=ALU.mult, op1=ALU.add,
                                       accum_out=ln_sum[:, tc, g:g + 1] if accumulate else None).then_inc(
                    drained[b], 1)
                fence()

            def layer_norm(scale, columns, gate=None, last=None):
                for tc in range(NT):
                    add_to_x(tc, 0, scale, gate, accumulate=True)

                def sums(tc):
                    add_to_x(tc, 1, scale, gate, accumulate=True)
                    v.tensor_scalar(ln_nmean[:, tc:tc + 1], ln_sum[:, tc, 0:1], ln_sum[:, tc, 1:2], -1.0 / D,
                                    ALU.add, ALU.mult).then_inc(y_ok, 1)
                    fence()

                def factors(tc):
                    col = slice(tc, tc + 1)
                    ve.wait_ge(sq_ok, n.up(sq_ok))
                    own(v.tensor_scalar(var[:, 0:1], ln_ssq[:, col], 1.0 / D, EPS, ALU.mult, ALU.add))
                    rsqrt_col(rstd[:, col], var[:, 0:1], newton[:, 0:2])

                if last is None:
                    for tc in range(NT):
                        if tc == 3:
                            modulated(0, *columns)
                        sums(tc)
                        factors(tc)
                        v.tensor_tensor(nmr[:, tc:tc + 1], ln_nmean[:, tc:tc + 1], rstd[:, tc:tc + 1],
                                        ALU.mult).then_inc(rs_ok, 1)
                        fence()
                    return

                def output(tc):
                    ve.wait_ge(xn_ok, n.up(xn_ok))
                    v.tensor_tensor(x[:, tc, :], x[:, tc, :], last[:, 0, :], ALU.mult).then_inc(gain_ok, 1)
                    if tc == NT - 1:
                        ve.wait_ge(gain_ok, n.at(gain_ok, NT))
                        v.tensor_tensor(x[:, tc, :], x[:, tc, :], last[:, 1, :], ALU.add).then_inc(last_ready, 1)

                ve.wait_ge(ln_in, n.up(ln_in, 32))
                n.skip(xn_ok, NT * (2 + 2 * LAYERS))
                for tc in range(NT):
                    if tc > 1:
                        output(tc - 2)
                    sums(tc)
                    factors(tc)
                    v.tensor_tensor(nmr[:, tc:tc + 1], ln_nmean[:, tc:tc + 1], rstd[:, tc:tc + 1],
                                    ALU.mult).then_inc(rs_ok, 1)
                    fence()
                output(NT - 2)
                output(NT - 1)

            def gain_and_bias(params, chunks=range(NT)):
                for tc in chunks:
                    own(v.tensor_tensor(x[:, tc, :], x[:, tc, :], params[:, 0, :], ALU.mult))
                    v.tensor_tensor(x[:, tc, :], x[:, tc, :], params[:, 1, :], ALU.add).then_inc(v_did, 1)
                    ve.wait_ge(v_did, n.up(v_did))
                    if tc == NT - 1:
                        ve.sem_inc(aff_ok, 1)

            def with_modulation(slot, index):
                ve.wait_ge(col_in, n.at(col_in))
                one_more, shift = mod_col[:, index, 8:16], mod_col[:, index, 0:8]
                gain, bias = (use_col[:, i:i + 1, :] for i in range(2))
                own(v.tensor_tensor(gain, ln_col[:, slot, 0:1, :], one_more, ALU.mult))
                own(v.tensor_tensor(bias, ln_col[:, slot, 1:2, :], one_more, ALU.mult))
                v.tensor_tensor(bias, bias, shift, ALU.add).then_inc(col_ok, 1)
                fence()

            v.memset(zero[:, :], 0.0).then_inc(zero_ok, 1)
            for b in range(8):
                ve.sem_inc(drained[b], 1)
            ve.sem_inc(mod_used, MOD_SLOTS)
            ve.sem_inc(sil_used, 2)
            for half_in in x_in:
                ve.wait_ge(half_in, 32)
                ve.sem_inc(xn_ok, 2)
            ve.wait_ge(col_in, 16)
            before_stage = use_col[:, 0, :], use_col[:, 1, :]
            modulated(0, *before_stage)
            own(v.memset(ones[:, :], 1.0))
            own(v.memset(mod_col[:, 0, 0:8], 0.0))
            own(v.memset(mod_col[:, 0, 8:16], 1.0))
            own(v.memset(ln_p[:, 0, :], 1.0))
            own(v.memset(ln_p[:, 1, :], 0.0))
            for w in (wf_hi, wf_lo, wa_hi, wa_lo):
                own(v.memset(w[:, :].bitcast(F32), 0.0))
            ve.wait_ge(ident_in, 16)
            ve.wait_ge(const_in, 16 * 4)
            own(v.tensor_copy(ident_b[:, :], ident[:, :]))
            v.tensor_copy(mask_b[:, :], tmp[:, 0:P]).then_inc(const_ok, 1)
            ve.wait_ge(modp_in, 16 * 5)
            own(v.tensor_copy(wa_hi[:, 0:KD * GLA_RANK], wa_raw[:, :]))
            v.tensor_tensor(wa_lo[:, 0:KD * GLA_RANK], wa_raw[:, :], wa_hi[:, 0:KD * GLA_RANK].bitcast(F32),
                            ALU.subtract).then_inc(wa_ok, 1)
            ve.wait_ge(cs_ok, 1)
            n.skip(col_in, 16)
            with n.loop(ve, LAYERS) as layer:
                modulated(1, *before_stage)
                ve.wait_ge(lay_in, n.up(lay_in, 16 * 4))
                own(v.tensor_copy(wf_hi[:, 0:KD * FOX_H], wf_raw[:, :]))
                v.tensor_tensor(wf_lo[:, 0:KD * FOX_H], wf_raw[:, :], wf_hi[:, 0:KD * FOX_H].bitcast(F32),
                                ALU.subtract).then_inc(wf_ok, 1)
                ve.wait_ge(f_log, n.up(f_log))
                fe, fm = P_f[0:FOX_H, 0:S], P_f[0:FOX_H, S:2 * S]
                own(v.tensor_scalar(fm, PS[0:FOX_H, 0, :], b_forget[:, 0:1], 0.0, ALU.add, ALU.min))
                ve.sem_inc(drained[0], 1)
                own(v.tensor_tensor(fm, fm, fe, ALU.subtract))
                own(v.tensor_tensor_scan(fe, ones[0:FOX_H, 0:1].broadcast_to([FOX_H, S]), fm, 0.0,
                                         ALU.mult, ALU.add))
                v.tensor_scalar(fm, fe, -1.0 / FOX_SCALE, None, ALU.mult).then_inc(c_ok, 1)
                for u in range(4):
                    b = 4 + u
                    bank(b)
                    v.tensor_copy(kT[:, u, :], PS[:, b, :]).then_inc(drained[b], 1)
                gain_and_bias(ln_p)

                def pair_out(c):
                    bank(7)
                    own(v.tensor_copy(mix_hi[:, c, :], PS[:, 7, :]))
                    v.tensor_tensor(mix_lo[:, c, :], PS[:, 7, :], mix_hi[:, c, :].bitcast(F32),
                                    ALU.subtract).then_inc(drained[7], 1)

                def rotate(src, chunks):
                    for tc in chunks:
                        s3 = src[:, tc, :].rearrange("p (h e) -> p h e", e=RET_D)
                        t3 = tmp[:, :].rearrange("p (h e) -> p h e", e=RET_D)
                        e = RET_D // 2
                        own(v.tensor_tensor(t3[:, :, 0:e], s3[:, :, e:], over(sin_t[:, tc, 0, :], RET_H), ALU.mult))
                        own(v.tensor_tensor(t3[:, :, e:], s3[:, :, 0:e], over(sin_t[:, tc, 1, :], RET_H), ALU.mult))
                        own(v.tensor_tensor(src[:, tc, :].rearrange("p (h e) -> p h e", e=e),
                                            src[:, tc, :].rearrange("p (h e) -> p h e", e=e),
                                            over(cos_t[:, tc, :], 2 * RET_H), ALU.mult))
                        v.tensor_tensor(src[:, tc, :], src[:, tc, :], tmp[:, :], ALU.add).then_inc(rot_ok, 1)
                        fence()

                ROTATIONS = {(3, "beside"): (("q", 0),), (5, "beside"): (("q", 1),),
                             (6, "after"): (("q", 2), ("q", 3)), (7, "beside"): (("k", 0),),
                             (7, "after"): (("k", 1), ("k", 2), ("k", 3))}

                def rotations(h, when):
                    for which, tc in ROTATIONS.get((h, when), ()):
                        if tc == 0:
                            ve.wait_ge(ret_raw, n.up(ret_raw))
                        rotate(rq if which == "q" else rk, (tc,))

                for h in range(FOX_H):
                    ve.wait_ge(cb_in[h % 2], n.up(cb_in[h % 2], 16))
                    for i in range(NT):
                        b, w = fox_bank(h, i), P * (i + 1)
                        bank(b)
                        settled()
                        v.tensor_tensor_reduce(out=P_f[:, ROW_OFF[i]:ROW_OFF[i] + w], in0=PS[:, b, 0:w],
                                               in1=cneg[:, h % 2, 0:w], scale=1.0, scalar=-3.0e38, op0=ALU.add,
                                               op1=ALU.max, accum_out=row_max[:, i:i + 1]).then_inc(drained[b], 1)
                    fence()
                    v.tensor_scalar(neg_max, row_max, -FOX_SCALE, None, ALU.mult).then_inc(max_ok, 1)
                    if h and h % 2 == 0:
                        pair_out(h // 2 - 1)
                    rotations(h, "beside")
                    ve.wait_ge(exp_ok, n.up(exp_ok, NT))
                    own(v.reciprocal(row_inv, row_sum))
                    for i in range(NT):
                        rows = P_f[:, ROW_OFF[i]:ROW_OFF[i] + P * (i + 1)]
                        v.tensor_scalar(rows, rows, row_inv[:, i:i + 1], None, ALU.mult).then_inc(p_ok, 1)
                    rotations(h, "after")
                    b = fox_bank(h, NT + 1)
                    bank(b)
                    v.tensor_copy(PT[:, 0:3, 2 * P:3 * P], four(b)[:, 0:3, :]).then_inc(drained[b], 1)
                pair_out(FOX_H // 2 - 1)
                for h in range(RET_H):
                    b = 4 + h
                    bank(b)
                    v.tensor_copy(qT[:, h, :], PS[:, b, :]).then_inc(drained[b], 1)

                def decayed(h):
                    for b, blocks in RET_BANKS:
                        bank(b)
                        at = 0
                        for j in blocks:
                            w = S - j * P
                            v.tensor_tensor(inner[h % 2][:, COL_OFF[j]:COL_OFF[j] + w], PS[:, b, at:at + w],
                                            decay[:, h, 0:w], ALU.mult).then_inc(inner_ok, 1)
                            at += w
                        ve.drain().then_inc(drained[b], 1)

                def group_stats(h):
                    ve.wait_ge(o_ok, n.up(o_ok))
                    settled()
                    for tc in range(NT):
                        v.bn_stats(gn_stats[:, tc, :], rq[:, tc, chunk(h)])
                    fence()
                    settled()
                    for tc in range(NT):
                        v.bn_aggr(gn_mv[:, tc, h, :], gn_stats[:, tc, :])
                    fence()

                decayed(0)
                for h in range(RET_H):
                    if h + 1 < RET_H:
                        decayed(h + 1)
                    else:
                        ve.wait_ge(ret_raw, n.up(ret_raw, 2))
                        own(v.tensor_tensor(rg[:, :, :], rg[:, :, :], over(gn_g[:, :], NT), ALU.mult))
                    group_stats(h)
                own(v.tensor_scalar(var.rearrange("p (t h) -> p t h", h=RET_H), gn_mv[:, :, :, 1], EPS, None,
                                    ALU.add))
                rsqrt(rstd, var, newton)
                v.scalar_tensor_tensor(out=gn_nmr.rearrange("p (t h) -> p t h", h=RET_H), in0=gn_mv[:, :, :, 0],
                                       scalar=-1.0, in1=rstd.rearrange("p (t h) -> p t h", h=RET_H),
                                       op0=ALU.mult, op1=ALU.mult).then_inc(gn_ok, 1)
                for tc in range(NT):
                    if tc % 2:
                        ve.wait_ge(gn_done, n.up(gn_done))
                    else:
                        for h in range(RET_H):
                            v.tensor_scalar(rq[:, tc, chunk(h)], rq[:, tc, chunk(h)], gn_mv[:, tc, h, 0:1],
                                            rstd[:, 4 * tc + h:4 * tc + h + 1], ALU.subtract, ALU.mult)
                        fence()
                    v.tensor_tensor(rq[:, tc, :], rq[:, tc, :], rg[:, tc, :], ALU.mult).then_inc(ret_ok, 1)
                for tc in range(NT):
                    b = 4 + tc
                    ve.wait_ge(hi_ok, n.up(hi_ok))
                    v.tensor_tensor(xT_lo[:, 4:8, chunk(tc)], four(b), xT_hi[:, 4:8, chunk(tc)].bitcast(F32),
                                    ALU.subtract).then_inc(drained[b], 1)
                n.skip(col_in, 32)
                ve.wait_ge(col_in, n.at(col_in))
                mid_layer = ln_col[:, 0, 0], ln_col[:, 0, 1]
                layer_norm(ALPHA_1, mid_layer)
                modulated(1, *mid_layer)

                def hidden(b, u, dst):
                    ve.wait_ge(relu_ok, n.up(relu_ok))
                    own(v.tensor_tensor(tmp[:, :], PS[:, b, :], relu_t[:, u % 2, :], ALU.mult))
                    ve.sem_inc(drained[b], 1)
                    own(v.tensor_copy(hid_hi[:, dst, :], tmp[:, :].unsqueeze(1)))
                    v.tensor_tensor(hid_lo[:, dst, :], tmp[:, :].unsqueeze(1),
                                    hid_hi[:, dst, :].bitcast(F32), ALU.subtract).then_inc(hid_ok, 1)
                    fence()

                ve.wait_ge(ln_in, n.up(ln_in, 32))
                for u in range(RING):
                    hidden(4 + u, u, slice(u, u + 1))
                    gain_and_bias(ln_p, (u,))
                for part in range(2):
                    settled()
                    with n.loop(ve, KF // RING - (part == 0)) as i:
                        for u in range(RING):
                            hidden(u, u, bass.ds(i * RING + (u + RING * (part == 0)), 1))
                    for g3 in range(3):
                        g = 3 * part + g3
                        for k in range(KD):
                            slot = (g * KD + k) % MOD_SLOTS
                            ve.wait_ge(mod_in[slot], n.up(mod_in[slot], 16))
                            if k == 0:
                                v.tensor_scalar(mod_acc[:, :], mod_raw[:, slot, :], c_col[:, 0:1], None,
                                                ALU.mult).then_inc(mod_used, 1)
                            else:
                                v.scalar_tensor_tensor(out=mod_acc[:, :], in0=mod_raw[:, slot, :],
                                                       scalar=c_col[:, k:k + 1], in1=mod_acc[:, :], op0=ALU.mult,
                                                       op1=ALU.add).then_inc(mod_used, 1)
                            fence()
                        bank(4)
                        if g < 4:
                            out = mod_col[:, bass.ds(layer + 1, 1), 4 * g:4 * g + 4]
                            v.scalar_tensor_tensor(out=out, in0=PS[:, 4, 0:4].unsqueeze(1),
                                                   scalar=float(g >= 2),
                                                   in1=mod_bias[:, bass.ds(layer, 1), 4 * g:4 * g + 4],
                                                   op0=ALU.add, op1=ALU.add).then_inc(drained[4], 1)
                        else:
                            out = gate1[:, bass.ds(layer, 1), half(g - 4)]
                            v.scalar_tensor_tensor(out=out, in0=PS[:, 4, :].unsqueeze(1), scalar=1.0, in1=out,
                                                   op0=ALU.add, op1=ALU.add).then_inc(drained[4], 1)
                    if part == 0:
                        for g in range(2):
                            for tc in range(NT):
                                add_to_x(tc, g, ALPHA_1)
                with_modulation(1, bass.ds(layer, 1))
                layer_norm(1.0, before_stage)
                ve.wait_ge(ln_in, n.up(ln_in, 32))

            v.memset(alrT[:, :], 1.0).then_inc(one_ok, 1)
            ve.wait_ge(one_ok, 1)
            modulated(1, *before_stage)
            bank(0)
            v.tensor_copy(alrT[0:GLA_RANK, :], PS[0:GLA_RANK, 0, :]).then_inc(drained[0], 1)
            for u in range(4):
                b = 4 + u
                bank(b)
                v.tensor_copy(gk[:, u, :], PS[:, b, :]).then_inc(drained[b], 1)
            gain_and_bias(ln_p)
            ve.wait_ge(la_log, n.up(la_log))
            for tc in range(NT):
                own(v.scalar_tensor_tensor(out=la[:, tc, :], in0=PS[:, tc, :], scalar=0.0, in1=la[:, tc, :],
                                           op0=ALU.min, op1=ALU.subtract))
                ve.sem_inc(drained[tc], 1)
                ve.drain().then_inc(la_ok, 1)
            for h in range(GLA_H):
                b = 4 + h % 2
                b3 = bT[:, :].rearrange("p (c s) -> p c s", s=GLA_C)
                bank(b)
                own(v.tensor_copy(bT[:, :], PS[:, b, :]))
                ve.sem_inc(drained[b], 1)
                v.tensor_tensor(kdT[:, h, :].rearrange("p (c s) -> p c s", s=GLA_C),
                                b3[:, :, GLA_C - 1:GLA_C].broadcast_to([P, NC, GLA_C]), b3,
                                ALU.subtract).then_inc(b_ok, 1)
                ve.wait_ge(e_ok, n.up(e_ok))
                v.tensor_tensor(gq[:, h, :], gq[:, h, :], e_pos[:, :], ALU.mult)
                own(v.tensor_tensor(kdT[:, h, :], kdT[:, h, :], gk[:, h, :], ALU.mult))
                v.tensor_tensor(gk[:, h, :], gk[:, h, :], e_neg[:, :], ALU.mult).then_inc(qk_ok, 1)
            ve.wait_ge(g_in, 16 * 3)

            def gla_out(tc):
                ve.wait_ge(gsq_ok, n.up(gsq_ok))
                cols = slice(0, GLA_H)
                own(v.tensor_scalar(var[:, cols], gla_ssq[:, tc % 2, :], 1.0 / GLA_DV, EPS, ALU.mult, ALU.add))
                rsqrt(rstd[:, cols], var[:, cols], newton[:, cols])
                for h in range(GLA_H):
                    b, cols = 2 * (tc % 2) + h // 2, slice((h % 2) * GLA_DV, (h % 2 + 1) * GLA_DV)
                    ins = v.scalar_tensor_tensor(out=go[:, tc, h * GLA_DV:(h + 1) * GLA_DV], in0=PS[:, b, cols],
                                                 scalar=rstd[:, h:h + 1], in1=norm_g[:, :], op0=ALU.mult,
                                                 op1=ALU.mult)
                    if h % 2:
                        ins.then_inc(drained[b], 1)
                fence()

            def masked_scores(c):
                b, r = GLA_BANK[c % 2], GLA_C * (c % 2)
                rows = slice(r, r + GLA_C)
                bank(b)
                v.tensor_tensor(att[rows, :, :], PS[rows, b, 0:GLA_H * GLA_C].rearrange("p (h i) -> p h i", i=GLA_C),
                                over(same_chunk[rows, r:r + GLA_C], GLA_H), ALU.mult).then_inc(att_ok, 1)
                ve.drain().then_inc(drained[b], 1)

            masked_scores(0)
            for c in range(NC):
                if c + 1 < NC:
                    masked_scores(c + 1)
                if c < NC - 1:
                    for b in (5, 6):
                        bank(b)
                        for h in (2 * (b - 5), 2 * (b - 5) + 1):
                            src = PS[:, b, (h % 2) * GLA_DV:(h % 2 + 1) * GLA_DV]
                            out = state[:, (c + 1) % 2, h, :]
                            if c == 0:
                                ins = v.tensor_copy(out, src)
                            else:
                                ins = v.scalar_tensor_tensor(out=out, in0=state[:, c % 2, h, :],
                                                             scalar=e_end[:, h, c:c + 1], in1=src,
                                                             op0=ALU.mult, op1=ALU.add)
                        ins.then_inc(drained[b], 1)
                    ve.drain().then_inc(st_ok, 1)
                    fence()
                if c % 2 == 0 and c:
                    gla_out(c // 2 - 1)
            gla_out(NT - 1)
            for g in range(2):
                for tc in range(NT):
                    b = 4 * (1 - g) + tc
                    ve.wait_ge(sil_ok, n.up(sil_ok))
                    out = go[:, tc, half(g)]
                    v.tensor_tensor(out, out, sil[:, tc % 2, :], ALU.mult).then_inc(sil_used, 1)
                    ve.drain().then_inc(drained[b], 1)
                    ve.drain().then_inc(go_ok, 1)
                for tc in range(NT):
                    hi, lo = (xT[:, 4:8, chunk(tc)] if g else gT[:, :, chunk(tc)]
                              for xT, gT in ((xT_hi, gT_hi), (xT_lo, gT_lo)))
                    ve.wait_ge(hi_ok, n.up(hi_ok))
                    v.tensor_tensor(lo, four(4 + tc), hi.bitcast(F32), ALU.subtract).then_inc(drained[4 + tc], 1)
            n.skip(col_in, 16)
            with_modulation(0, slice(2, 3))
            layer_norm(ALPHA_2, before_stage, gate1[:, 0, :])
            modulated(1, *before_stage)
            ve.wait_ge(ln_in, n.up(ln_in, 32))
            own(v.memset(u_pad[:, 0:2], 0.0))

            def gated(u, f, dst):
                ve.wait_ge(u_ok, n.up(u_ok))
                taps = [conv[:, f, j] for j in range(4)]
                own(v.tensor_scalar(u_conv[:, 1, :], u_pad[:, 2:2 + S], taps[2], taps[3], ALU.mult, ALU.add))
                own(v.scalar_tensor_tensor(out=u_conv[:, 1, :], in0=u_pad[:, 1:1 + S], scalar=taps[1],
                                           in1=u_conv[:, 1, :], op0=ALU.mult, op1=ALU.add))
                v.scalar_tensor_tensor(out=u_conv[:, 1, :], in0=u_pad[:, 0:S], scalar=taps[0],
                                       in1=u_conv[:, 1, :], op0=ALU.mult, op1=ALU.add).then_inc(cv_ok, 1)
                ve.drain().then_inc(drained[4 + 2 * u], 1)
                ve.wait_ge(su_ok, n.up(su_ok))
                bank(5 + 2 * u)
                own(v.tensor_tensor(tmp[:, :], PS[:, 5 + 2 * u, :], u_conv[:, 0, :], ALU.mult))
                ve.sem_inc(drained[5 + 2 * u], 1)
                own(v.tensor_copy(hid2_hi[:, dst, :], tmp[:, :].unsqueeze(1)))
                v.tensor_tensor(hid2_lo[:, dst, :], tmp[:, :].unsqueeze(1),
                                hid2_hi[:, dst, :].bitcast(F32), ALU.subtract).then_inc(hid_ok, 1)
                fence()

            for u in range(2):
                gated(u, slice(u, u + 1), slice(u, u + 1))
                gain_and_bias(ln_p2, (2 * u, 2 * u + 1))
            done = 0
            for part, kf in enumerate(KF2):
                first = 2 * (part == 0)
                with n.loop(ve, kf // 2 - (part == 0)) as i:
                    for u in range(2):
                        gated(u, bass.ds(i * 2 + (u + done + first), 1), bass.ds(i * 2 + (u + first), 1))
                done += kf
                if part == 0:
                    for g in range(2):
                        for tc in range(NT):
                            add_to_x(tc, g, ALPHA_2, gate1[:, 1, :])
            layer_norm(1.0, None, gate1[:, 1, :], last=ln_p2)


def tables():
    f32 = np.float32
    p = np.arange(P)
    inv_freq = f32(10000.0) ** (-np.arange(RET_D // 2, dtype=f32) / f32(RET_D // 2))
    angle = (np.arange(S, dtype=f32)[:, None] * inv_freq[None, :]).astype(f32).astype(np.float64)
    cos, sin = (f(angle).astype(f32).reshape(NT, P, RET_D // 2).transpose(1, 0, 2) for f in (np.cos, np.sin))
    gamma = 1.0 - 2.0 ** (-5.0 - np.arange(RET_H))
    steps = np.arange(S)[None, :] - p[:, None]
    decay = np.where(steps >= 0, gamma[:, None, None] ** np.maximum(steps, 0), 0.0) * RET_D ** -0.5
    return {
        "ident": np.eye(P, dtype=f32),
        "causal": np.where(p[None, :] <= p[:, None], 0.0, MASKED).astype(f32),
        "same_chunk": ((p[:, None] <= p[None, :]) & (p[:, None] // GLA_C == p[None, :] // GLA_C)).astype(f32),
        "cos": np.ascontiguousarray(cos),
        "sin": np.ascontiguousarray(np.stack([-sin, sin], 2)),
        "decay": np.ascontiguousarray(decay.transpose(1, 0, 2).astype(f32)),
    }


def across_units(w):
    return w.reshape(KD, P, -1, P).transpose(2, 1, 0, 3).reshape(-1, P, UNIT)


def down_units(w):
    return w.reshape(-1, 2, P, w.shape[1] // HALF, HALF).transpose(3, 0, 2, 1, 4).reshape(-1, P, UNIT)


def narrow_weights(w):
    return np.ascontiguousarray(w.reshape(KD, P, -1).transpose(1, 0, 2).reshape(P, -1))


def lay_out(a):
    fox, ret = FOX_H * FOX_D, RET_H * RET_D
    units, forget = [], []
    for i in range(LAYERS):
        w = a["w_in"][i]
        units.append(across_units(w[:, :2 * fox]))
        units.append(down_units(w[:, 2 * fox:3 * fox]))
        forget.append(narrow_weights(w[:, 3 * fox:3 * fox + FOX_H]))
        units.append(down_units(w[:, 3 * fox + FOX_H:]))
        units.append(down_units(a["w_out"][i]))
        part = KF * P
        for j in range(2):
            units.append(across_units(a["w_ff1"][i][:, j * part:(j + 1) * part]))
            units.append(down_units(a["w_ff2"][i][j * part:(j + 1) * part]))
    w = a["gla_w_in_2"][0]
    qk, dv = GLA_H * GLA_DK, GLA_H * GLA_DV
    units.append(across_units(w[:, :2 * qk]))
    units.append(down_units(w[:, 2 * qk:2 * qk + 2 * dv]))
    units.append(down_units(a["gla_w_o_2"][0]))
    up = across_units(a["ffn_w_up_2"][0]).reshape(2, FF2 // P, P, UNIT).transpose(1, 0, 2, 3)
    at = 0
    for kf in KF2:
        units.append(up[at:at + kf].reshape(-1, P, UNIT))
        units.append(down_units(a["ffn_w_down_2"][0][at * P:(at + kf) * P]))
        at += kf
    mod_b = a["mod_b_2"][0]
    taps = np.concatenate([a["ffn_conv_w_2"][0], a["ffn_conv_b_2"]], 0)
    cols = [(np.ones(D, np.float32), np.zeros(D, np.float32))]
    for i in range(LAYERS):
        cols += [(a["ln1_g"][i], a["ln1_b"][i]), (a["ln2_g"][i], a["ln2_b"][i])]
    cols.append((a["ln_g_2"][0, 0], a["ln_b_2"][0, 0]))
    laid = {
        "ln_cols": np.stack([np.stack(c) for c in cols]).reshape(-1, 2, KD, P).transpose(0, 3, 1, 2),
        "x": a["x"][0],
        "stream": np.concatenate(units, 0),
        "w_forget": np.stack(forget),
        "b_forget": a["b_forget"][:, :, None],
        "gn_g": a["ret_gn_g"].reshape(LAYERS, 1, ret),
        "c": a["c_2"][0].reshape(KD, P).T,
        "mod": a["mod_w_2"][0].reshape(2, KD, P, MOD_GROUPS, HALF).transpose(0, 3, 1, 2, 4),
        "mod_bias": mod_b[:, :2 * D].reshape(2, 16, P).transpose(2, 0, 1),
        "gate_bias": mod_b[:, 2 * D:],
        "conv": taps.reshape(4, FF2 // P, P).transpose(2, 1, 0),
        "w_a": narrow_weights(w[:, 2 * qk + 2 * dv:]),
        "w_a2": a["gla_w_a2_2"][0],
        "b_a": a["gla_b_a_2"],
        "norm_g": a["gla_norm_g_2"],
        "ln_g_2": a["ln_g_2"][0],
        "ln_b_2": a["ln_b_2"][0],
    }
    for name in ("ln1_g", "ln1_b", "ln2_g", "ln2_b"):
        laid[name] = a[name][:, None, :]
    return {k: np.ascontiguousarray(v) for k, v in laid.items()}


def add_program(nc, shapes, per_turn):
    t = {k: nc.dram_tensor(f"in_{k}", s, F32, kind="ExternalInput").ap() for k, s in shapes.items()}
    out = nc.dram_tensor("out", (S, D), F32, kind="ExternalOutput").ap()
    t["out"] = out.rearrange("(t p) d -> t p d", p=P)
    t["x"] = t["x"].rearrange("(t p) d -> p t d", p=P)
    t["gate_bias"] = t["gate_bias"].unsqueeze(0).broadcast_to([P, 2, D])
    t["c_scratch"] = nc.dram_tensor("c_scratch", (FOX_H, S), F32, kind="Internal").ap()
    program(nc, t, per_turn)


def kernel(**inputs):
    import concourse.bacc as bacc
    from concourse.bass_utils import run_bass_kernel_spmd

    arrays = {**lay_out({k: np.asarray(v) for k, v in inputs.items()}), **tables()}
    shapes = {k: v.shape for k, v in arrays.items()}
    per_turn = {}
    for _ in range(2):
        nc = bacc.Bacc("TRN2", target_bir_lowering=False, num_devices=1)
        add_program(nc, shapes, per_turn)
    r = run_bass_kernel_spmd(nc, [{f"in_{k}": v for k, v in arrays.items()}], core_ids=[0])
    return r.results[0]["out"].reshape(1, S, D)
```
